# Optimizing a Trainium2 kernel written in Bass

```python
import jax, jax.numpy as jnp
from jax import lax
import numpy as np

D_MODEL = 1024
BATCH = 1
SEQ = 512
DEPTH = 1

HEAD_DIM = 64
ROPE_DIM = HEAD_DIM // 4
ROPE_THETA = 500000.0
Q_BLOCK = 128
EPS = 1e-6
NEG_INF = -1e30
FORCED_SCORE = 1e6
NSA_HEADS = 8
NSA_KV_HEADS = 2
NSA_GROUP = NSA_HEADS // NSA_KV_HEADS
CMP_LEN = 32
CMP_STRIDE = 16
CMP_HIDDEN = 128
SLC_BLOCK = 64
SLC_TOPN = 8
WINDOW = 512
DSA_HEADS = 8
KV_LORA = 128
NOPE_DIM = HEAD_DIM - ROPE_DIM
IDX_HEADS = 8
IDX_DIM = 64
IDX_TOPK_MAX = 256
D_FF = ((8 * D_MODEL + 3 * 256 - 1) // (3 * 256)) * 256
IN_SPLITS = (NSA_HEADS * HEAD_DIM,) + (NSA_KV_HEADS * HEAD_DIM,) * 6 + (
    3 * NSA_HEADS, DSA_HEADS * HEAD_DIM, KV_LORA, ROPE_DIM, IDX_HEADS * IDX_DIM, IDX_DIM, IDX_HEADS)
IN_WIDTH = sum(IN_SPLITS)


def _rms_norm(x, g):
    xf = x.astype(jnp.float32)
    y = xf * lax.rsqrt(jnp.mean(xf * xf, axis=-1, keepdims=True) + EPS)
    return (y * g.astype(jnp.float32)).astype(x.dtype)

def _rope_tables(seq):
    inv_freq = 1.0 / (ROPE_THETA ** (jnp.arange(0, ROPE_DIM, 2, dtype=jnp.float32) / ROPE_DIM))
    ang = jnp.arange(seq, dtype=jnp.float32)[:, None] * inv_freq[None, :]
    return jnp.cos(ang), jnp.sin(ang)

def _rope(x, cos, sin):
    half = ROPE_DIM // 2
    xr = x[..., :ROPE_DIM].astype(jnp.float32)
    x1, x2 = xr[..., :half], xr[..., half:]
    c, s = cos[:, None, :], sin[:, None, :]
    rot = jnp.concatenate([x1 * c - x2 * s, x2 * c + x1 * s], axis=-1)
    return jnp.concatenate([rot.astype(x.dtype), x[..., ROPE_DIM:]], axis=-1)

def _masked_softmax(s, mask):
    s = jnp.where(mask, s.astype(jnp.float32), NEG_INF)
    m = jnp.max(s, axis=-1, keepdims=True)
    e = jnp.where(mask, jnp.exp(s - m), 0.0)
    return e / jnp.maximum(jnp.sum(e, axis=-1, keepdims=True), 1e-30)

def _q_blocks(a):
    b, s = a.shape[:2]
    return jnp.moveaxis(a.reshape((b, s // Q_BLOCK, Q_BLOCK) + a.shape[2:]), 1, 0)

def _from_blocks(o):
    nb, b, tq = o.shape[:3]
    return jnp.moveaxis(o, 0, 1).reshape((b, nb * tq) + o.shape[3:])

def _compress(k, pe, w1, b1, w2, b2):
    b, s, g, dh = k.shape
    n_cmp = (s - CMP_LEN) // CMP_STRIDE + 1
    idx = np.arange(n_cmp)[:, None] * CMP_STRIDE + np.arange(CMP_LEN)[None, :]
    blocks = k[:, idx] + pe[:, None, :]
    flat = jnp.transpose(blocks, (0, 3, 1, 2, 4)).reshape(b, g, n_cmp, CMP_LEN * dh)
    hid = jax.nn.gelu(flat @ w1 + b1)
    return hid @ w2 + b2

def _nsa_group(q, k_cmp, v_cmp, k_slc, v_slc, k_win, v_win, gates, cos, sin,
               cmp_pe, cmp_w1, cmp_b1, cmp_w2, cmp_b2):
    b, s = q.shape[:2]
    g_, r_, dh = NSA_KV_HEADS, NSA_GROUP, HEAD_DIM
    scale = HEAD_DIM ** -0.5
    tpos = jnp.arange(s)
    qg = _rope(q.reshape(b, s, NSA_HEADS, dh), cos, sin).reshape(b, s, g_, r_, dh)
    kc = _compress(_rope(k_cmp.reshape(b, s, g_, dh), cos, sin), cmp_pe[0], cmp_w1[0], cmp_b1[0], cmp_w2[0], cmp_b2[0])
    vc = _compress(v_cmp.reshape(b, s, g_, dh), cmp_pe[1], cmp_w1[1], cmp_b1[1], cmp_w2[1], cmp_b2[1])
    n_cmp = kc.shape[2]
    cmp_end = jnp.arange(n_cmp) * CMP_STRIDE + CMP_LEN - 1
    mask_c = cmp_end[None, :] <= tpos[:, None]
    p_c = _masked_softmax(jnp.einsum('bsgrd,bgnd->bgrsn', qg, kc) * scale, mask_c)
    o_cmp = jnp.einsum('bgrsn,bgnd->bsgrd', p_c.astype(vc.dtype), vc).reshape(b, s, NSA_HEADS, dh)
    n_slc = s // SLC_BLOCK
    ci = np.arange(n_cmp)[:, None] * CMP_STRIDE
    sj = np.arange(n_slc)[None, :] * SLC_BLOCK
    overlap = ((ci < sj + SLC_BLOCK) & (ci + CMP_LEN > sj)).astype(np.float32)
    imp = jnp.einsum('bgrsn,nj->bgsj', p_c, jnp.asarray(overlap))
    blk_t = (tpos // SLC_BLOCK)[:, None]
    j = jnp.arange(n_slc)[None, :]
    visible = j <= blk_t
    forced = (j == 0) | (j == blk_t) | (j == blk_t - 1)
    imp = jnp.where(visible, jnp.where(forced, FORCED_SCORE, imp), -jnp.inf)
    n_sel = min(SLC_TOPN, n_slc)
    _, sel = lax.top_k(imp, n_sel)
    ks_blocks = jnp.transpose(_rope(k_slc.reshape(b, s, g_, dh), cos, sin).reshape(b, n_slc, SLC_BLOCK, g_, dh), (0, 3, 1, 2, 4))
    vs_blocks = jnp.transpose(v_slc.reshape(b, n_slc, SLC_BLOCK, g_, dh), (0, 3, 1, 2, 4))
    pad = ((0, 0), (WINDOW, 0), (0, 0), (0, 0))
    kw = jnp.pad(_rope(k_win.reshape(b, s, g_, dh), cos, sin), pad)
    vw = jnp.pad(v_win.reshape(b, s, g_, dh), pad)
    gather = jax.vmap(jax.vmap(lambda tab, ix: tab[ix]))

    def block_fn(args):
        q_b, sel_b, t0 = args
        sel_b = jnp.transpose(sel_b, (0, 2, 1, 3))
        tq = t0 + jnp.arange(Q_BLOCK)
        kg = gather(ks_blocks, sel_b).reshape(b, g_, Q_BLOCK, n_sel * SLC_BLOCK, dh)
        vg = gather(vs_blocks, sel_b).reshape(b, g_, Q_BLOCK, n_sel * SLC_BLOCK, dh)
        kpos = (sel_b[..., None] * SLC_BLOCK + jnp.arange(SLC_BLOCK)).reshape(b, g_, Q_BLOCK, n_sel * SLC_BLOCK)
        mask_s = (kpos <= tq[None, None, :, None])[:, :, None]
        p_s = _masked_softmax(jnp.einsum('btgrd,bgtkd->bgrtk', q_b, kg) * scale, mask_s)
        o_s = jnp.einsum('bgrtk,bgtkd->btgrd', p_s.astype(vg.dtype), vg)
        kwb = lax.dynamic_slice_in_dim(kw, t0, Q_BLOCK + WINDOW, axis=1)
        vwb = lax.dynamic_slice_in_dim(vw, t0, Q_BLOCK + WINDOW, axis=1)
        wpos = t0 - WINDOW + jnp.arange(Q_BLOCK + WINDOW)
        mask_w = (wpos[None, :] <= tq[:, None]) & (wpos[None, :] > tq[:, None] - WINDOW) & (wpos[None, :] >= 0)
        p_w = _masked_softmax(jnp.einsum('btgrd,bsgd->bgrts', q_b, kwb) * scale, mask_w)
        o_w = jnp.einsum('bgrts,bsgd->btgrd', p_w.astype(vwb.dtype), vwb)
        return o_s, o_w

    starts = jnp.arange(s // Q_BLOCK, dtype=jnp.int32) * Q_BLOCK
    o_s, o_w = lax.map(block_fn, (_q_blocks(qg), _q_blocks(jnp.transpose(sel, (0, 2, 1, 3))), starts))
    o_s = _from_blocks(o_s).reshape(b, s, NSA_HEADS, dh)
    o_w = _from_blocks(o_w).reshape(b, s, NSA_HEADS, dh)
    gt = jax.nn.sigmoid(gates.astype(jnp.float32)).astype(q.dtype).reshape(b, s, 3, NSA_HEADS, 1)
    o = gt[:, :, 0] * o_cmp + gt[:, :, 1] * o_s + gt[:, :, 2] * o_w
    return o.reshape(b, s, NSA_HEADS * dh)

def _dsa_group(q, c_kv, k_rope, q_idx, k_idx, w_idx, cos, sin, g_kv, w_uk, w_uv):
    b, s = q.shape[:2]
    scale = HEAD_DIM ** -0.5
    q = _rope(q.reshape(b, s, DSA_HEADS, HEAD_DIM), cos, sin)
    q_rope, q_nope = q[..., :ROPE_DIM], q[..., ROPE_DIM:]
    c_kv = _rms_norm(c_kv, g_kv)
    k_rope = _rope(k_rope[:, :, None, :], cos, sin)[:, :, 0]
    q_lat = jnp.einsum('bshe,hre->bshr', q_nope, w_uk)
    q_idx = _rope(q_idx.reshape(b, s, IDX_HEADS, IDX_DIM), cos, sin)
    k_idx = _rope(k_idx[:, :, None, :], cos, sin)[:, :, 0]
    w_idx = w_idx.astype(jnp.float32) * (IDX_HEADS ** -0.5 * IDX_DIM ** -0.5)
    k_sel = min(IDX_TOPK_MAX, s // 4)
    spos = jnp.arange(s)
    gather = jax.vmap(lambda tab, ix: tab[ix])

    def block_fn(args):
        ql_b, qr_b, qi_b, wi_b, t0 = args
        tq = t0 + jnp.arange(Q_BLOCK)
        logits = jnp.einsum('bthd,bsd->bths', qi_b, k_idx).astype(jnp.float32)
        score = jnp.einsum('bths,bth->bts', jax.nn.relu(logits), wi_b)
        score = jnp.where(spos[None, None, :] <= tq[None, :, None], score, -jnp.inf)
        _, idx = lax.top_k(score, k_sel)
        cg = gather(c_kv, idx)
        krg = gather(k_rope, idx)
        sc = (jnp.einsum('bthr,btkr->bhtk', ql_b, cg) + jnp.einsum('bthe,btke->bhtk', qr_b, krg)) * scale
        mask = (idx <= tq[None, :, None])[:, None]
        p = _masked_softmax(sc, mask)
        return jnp.einsum('bhtk,btkr->bthr', p.astype(cg.dtype), cg)

    starts = jnp.arange(s // Q_BLOCK, dtype=jnp.int32) * Q_BLOCK
    o_lat = _from_blocks(lax.map(block_fn, (_q_blocks(q_lat), _q_blocks(q_rope), _q_blocks(q_idx), _q_blocks(w_idx), starts)))
    o = jnp.einsum('bshr,hrd->bshd', o_lat, w_uv)
    return o.reshape(b, s, DSA_HEADS * HEAD_DIM)

def _hybrid_mixer(h, cos, sin, w_in, cmp_pe, cmp_w1, cmp_b1, cmp_w2, cmp_b2, g_kv, w_uk, w_uv, w_out):
    proj = h @ w_in
    split_points = [int(v) for v in np.cumsum(IN_SPLITS)[:-1]]
    (nq, nkc, nvc, nks, nvs, nkw, nvw, ngate, dq, dckv, dkr, iq, ik, iw) = jnp.split(proj, split_points, axis=-1)
    o_a = _nsa_group(nq, nkc, nvc, nks, nvs, nkw, nvw, ngate, cos, sin, cmp_pe, cmp_w1, cmp_b1, cmp_w2, cmp_b2)
    o_b = _dsa_group(dq, dckv, dkr, iq, ik, iw, cos, sin, g_kv, w_uk, w_uv)
    return jnp.concatenate([o_a, o_b], axis=-1) @ w_out

def _swiglu(h, w_gate_up, w_down):
    gate, up = jnp.split(h @ w_gate_up, 2, axis=-1)
    return (jax.nn.silu(gate) * up) @ w_down

def first_inputs(seed: int = 0) -> dict:
    key = jax.random.key(seed)
    ks = jax.random.split(key, 20)
    L = DEPTH

    def nrm(k, shape, scale):
        return jax.random.normal(k, shape, jnp.float32) * scale

    def gain(k, shape):
        return 1.0 + 0.05 * jax.random.normal(k, shape, jnp.float32)

    return {
        'x': nrm(ks[0], (BATCH, SEQ, D_MODEL), 1.0),
        'c': nrm(ks[1], (BATCH, D_MODEL), 1.0),
        'w_ada': nrm(ks[2], (L, D_MODEL, 6 * D_MODEL), 0.5 * D_MODEL ** -0.5),
        'b_ada': nrm(ks[3], (L, 6 * D_MODEL), 0.01),
        'g_pre_mix': gain(ks[4], (L, D_MODEL)),
        'g_post_mix': gain(ks[5], (L, D_MODEL)),
        'g_pre_ffn': gain(ks[6], (L, D_MODEL)),
        'g_post_ffn': gain(ks[7], (L, D_MODEL)),
        'w_in': nrm(ks[8], (L, D_MODEL, IN_WIDTH), D_MODEL ** -0.5),
        'cmp_pe': nrm(ks[9], (L, 2, CMP_LEN, HEAD_DIM), 0.1),
        'cmp_w1': nrm(ks[10], (L, 2, CMP_LEN * HEAD_DIM, CMP_HIDDEN), (CMP_LEN * HEAD_DIM) ** -0.5),
        'cmp_b1': nrm(ks[11], (L, 2, CMP_HIDDEN), 0.01),
        'cmp_w2': nrm(ks[12], (L, 2, CMP_HIDDEN, HEAD_DIM), CMP_HIDDEN ** -0.5),
        'cmp_b2': nrm(ks[13], (L, 2, HEAD_DIM), 0.01),
        'g_kv_norm': gain(ks[14], (L, KV_LORA)),
        'w_uk': nrm(ks[15], (L, DSA_HEADS, KV_LORA, NOPE_DIM), KV_LORA ** -0.5),
        'w_uv': nrm(ks[16], (L, DSA_HEADS, KV_LORA, HEAD_DIM), KV_LORA ** -0.5),
        'w_out': nrm(ks[17], (L, D_MODEL, D_MODEL), D_MODEL ** -0.5),
        'w_gate_up': nrm(ks[18], (L, D_MODEL, 2 * D_FF), D_MODEL ** -0.5),
        'w_down': nrm(ks[19], (L, D_FF, D_MODEL), D_FF ** -0.5),
    }

def first_block(x, c, w_ada, b_ada, g_pre_mix, g_post_mix, g_pre_ffn, g_post_ffn, w_in,
              cmp_pe, cmp_w1, cmp_b1, cmp_w2, cmp_b2, g_kv_norm, w_uk, w_uv, w_out,
              w_gate_up, w_down):
    cos, sin = _rope_tables(x.shape[1])
    c_act = jax.nn.silu(c)
    for l in range(DEPTH):
        mod = (c_act @ w_ada[l] + b_ada[l])[:, None, :]
        sh_m, sc_m, ga_m, sh_f, sc_f, ga_f = jnp.split(mod, 6, axis=-1)
        h = _rms_norm(x, g_pre_mix[l]) * (1.0 + sc_m) + sh_m
        y = _hybrid_mixer(h, cos, sin, w_in[l], cmp_pe[l], cmp_w1[l], cmp_b1[l], cmp_w2[l], cmp_b2[l],
                          g_kv_norm[l], w_uk[l], w_uv[l], w_out[l])
        x = x + ga_m * _rms_norm(y, g_post_mix[l])
        h = _rms_norm(x, g_pre_ffn[l]) * (1.0 + sc_f) + sh_f
        x = x + ga_f * _rms_norm(_swiglu(h, w_gate_up[l], w_down[l]), g_post_ffn[l])
    return x


CTX_LEN = 256
GRID_W = 64
N_MOD = 9
D_FF_2 = 2816
M_HEADS = 4
M_HD = 128
M_W = M_HEADS * M_HD
CONV_W = 3
CHUNK = 128
POOL_WINDOWS = (2, 4, 8, 16)
POOL_GROUPS = len(POOL_WINDOWS)
POOL_W = 512
POOL_GW = POOL_W // POOL_GROUPS
MIX_W = M_W + POOL_W
M_COLS = 3 * M_W + 4 * M_HEADS
IN_COLS = M_COLS + POOL_W


def rmsnorm(x, g):
    xf = x.astype(jnp.float32)
    y = xf * lax.rsqrt(jnp.mean(xf * xf, axis=-1, keepdims=True) + EPS)
    return (y * g.astype(jnp.float32)).astype(x.dtype)

def ada_in(x, mod, j, g):
    return rmsnorm(x, g) * (1 + mod[:, 3 * j + 1, None]) + mod[:, 3 * j, None]

def ada_out(x, z, mod, j, g, res_w):
    return x + res_w * mod[:, 3 * j + 2, None] * rmsnorm(z, g)

def swiglu(y, w_in, w_out):
    a, b = jnp.split(y @ w_in, 2, axis=-1)
    return (jax.nn.silu(a) * b) @ w_out

def centred_mean(u, win, axis):
    n = u.shape[axis]
    lo, hi = win // 2, win - 1 - win // 2
    pad = [(0, 0)] * u.ndim
    pad[axis] = (lo + 1, hi)
    s = jnp.cumsum(jnp.pad(u.astype(jnp.float32), pad), axis=axis)
    tot = lax.slice_in_dim(s, win, win + n, axis=axis) - lax.slice_in_dim(s, 0, n, axis=axis)
    t = jnp.arange(n)
    cnt = (jnp.minimum(t + hi, n - 1) - jnp.maximum(t - lo, 0) + 1).astype(jnp.float32)
    shape = [1] * u.ndim
    shape[axis] = n
    return (tot / cnt.reshape(shape)).astype(u.dtype)

def pool_mixer(u, w_pool, pool_scale, on_grid):
    bsz, n, _ = u.shape
    outs = []
    for gi, win in enumerate(POOL_WINDOWS):
        ug = u[..., gi * POOL_GW:(gi + 1) * POOL_GW]
        if on_grid:
            rows = n // GRID_W
            ug2 = ug.reshape(bsz, rows, GRID_W, POOL_GW)
            pg = centred_mean(centred_mean(ug2, win, 2), win, 1).reshape(bsz, n, POOL_GW)
        else:
            pg = centred_mean(ug, win, 1)
        outs.append(pg - ug)
    d = jnp.stack(outs, axis=2)
    y = jnp.einsum('bngc,gcd->bngd', d, w_pool).reshape(bsz, n, POOL_W)
    return y * pool_scale

def short_conv(u, w, b):
    n = u.shape[1]
    h = CONV_W // 2
    up = jnp.pad(u, ((0, 0), (h, h), (0, 0)))
    out = b
    for j in range(CONV_W):
        out = out + up[:, j:j + n] * w[j]
    return out

def mlstm_inputs(p, conv_w, conv_b, w_q, w_k, i_bias, f_bias):
    bsz, n, _ = p.shape
    u = jax.nn.silu(short_conv(p[..., :M_W], conv_w, conv_b)).reshape(bsz, n, M_HEADS, M_HD)
    q = jnp.einsum('bnhd,hde->bhne', u, w_q).astype(jnp.float32)
    k = jnp.einsum('bnhd,hde->bhne', u, w_k).astype(jnp.float32)
    v = p[..., M_W:2 * M_W].reshape(bsz, n, M_HEADS, M_HD).transpose(0, 2, 1, 3).astype(jnp.float32)
    g0 = 3 * M_W
    ig = (p[..., g0:g0 + 2 * M_HEADS].reshape(bsz, n, 2, M_HEADS) + i_bias).astype(jnp.float32)
    fg = (p[..., g0 + 2 * M_HEADS:M_COLS].reshape(bsz, n, 2, M_HEADS) + f_bias).astype(jnp.float32)
    return q, k, v, ig.transpose(2, 0, 3, 1), fg.transpose(2, 0, 3, 1)

def mlstm_chunkwise(q, k, v, i_pre, f_pre):
    bsz, nh, t_len, dk = q.shape
    nc = t_len // CHUNK
    q = q.reshape(bsz, nh, nc, CHUNK, dk)
    k = k.reshape(bsz, nh, nc, CHUNK, dk) * (dk ** -0.5)
    v = v.reshape(bsz, nh, nc, CHUNK, dk)
    ip = i_pre.reshape(bsz, nh, nc, CHUNK)
    b = jnp.cumsum(jax.nn.log_sigmoid(f_pre).reshape(bsz, nh, nc, CHUNK), axis=-1)
    g = b[..., -1]
    a = g[..., None] - b + ip
    m_loc = jnp.max(a, axis=-1)
    wk = jnp.exp(a - m_loc[..., None])[..., None] * k
    ckv = jnp.einsum('bhclk,bhclv->bhckv', wk, v)
    cn = jnp.sum(wk, axis=3)

    def step(carry, inp):
        c_st, n_st, m_st = carry
        g_c, m_c, ckv_c, cn_c = inp
        m_new = jnp.maximum(g_c + m_st, m_c)
        a_old = jnp.exp(g_c + m_st - m_new)
        a_new = jnp.exp(m_c - m_new)
        c_new = a_old[..., None, None] * c_st + a_new[..., None, None] * ckv_c
        n_new = a_old[..., None] * n_st + a_new[..., None] * cn_c
        return (c_new, n_new, m_new), (c_st, n_st, m_st)

    init = (jnp.zeros((bsz, nh, dk, dk), jnp.float32), jnp.zeros((bsz, nh, dk), jnp.float32),
            jnp.zeros((bsz, nh), jnp.float32))
    xs = (jnp.moveaxis(g, -1, 0), jnp.moveaxis(m_loc, -1, 0), jnp.moveaxis(ckv, 2, 0), jnp.moveaxis(cn, 2, 0))
    _, (c_in, n_in, m_in) = lax.scan(step, init, xs)
    c_in = jnp.moveaxis(c_in, 0, 2)
    n_in = jnp.moveaxis(n_in, 0, 2)
    m_in = jnp.moveaxis(m_in, 0, -1)
    mask = jnp.tril(jnp.ones((CHUNK, CHUNK), dtype=bool))
    dmat = jnp.where(mask, b[..., :, None] - b[..., None, :] + ip[..., None, :], -jnp.inf)
    inter = b + m_in[..., None]
    m_t = jnp.maximum(jnp.max(dmat, axis=-1), inter)
    s = jnp.einsum('bhctk,bhcsk->bhcts', q, k) * jnp.exp(dmat - m_t[..., None])
    w_inter = jnp.exp(inter - m_t)
    num = w_inter[..., None] * jnp.einsum('bhctk,bhckv->bhctv', q, c_in) + jnp.einsum('bhcts,bhcsv->bhctv', s, v)
    den = w_inter * jnp.einsum('bhctk,bhck->bhct', q, n_in) + jnp.sum(s, axis=-1)
    h = num / jnp.maximum(jnp.abs(den), jnp.exp(-m_t))[..., None]
    return h.reshape(bsz, nh, t_len, dk)

def mlstm_bidir(p_lat, p_ctx, conv_w, conv_b, w_q, w_k, i_bias, f_bias):
    ql, kl, vl, il, fl = mlstm_inputs(p_lat, conv_w, conv_b, w_q, w_k, i_bias, f_bias)
    qc, kc, vc, ic, fc = mlstm_inputs(p_ctx, conv_w, conv_b, w_q, w_k, i_bias, f_bias)
    lc = qc.shape[2]
    cat = lambda a, b: jnp.concatenate([a, b], axis=2)
    rev = lambda a: jnp.flip(a, axis=2)
    h_f = mlstm_chunkwise(cat(qc, ql), cat(kc, kl), cat(vc, vl), cat(ic[0], il[0]), cat(fc[0], fl[0]))
    h_b = mlstm_chunkwise(cat(rev(qc), rev(ql)), cat(rev(kc), rev(kl)), cat(rev(vc), rev(vl)),
                          cat(rev(ic[1]), rev(il[1])), cat(rev(fc[1]), rev(fl[1])))
    h_lat = h_f[:, :, lc:] + rev(h_b[:, :, lc:])
    h_ctx = h_f[:, :, :lc] + rev(h_b[:, :, :lc])
    return h_lat, h_ctx

def mlstm_out(h, o, g):
    bsz, _, n, _ = h.shape
    h = h.transpose(0, 2, 1, 3)
    h = h * lax.rsqrt(jnp.mean(h * h, axis=-1, keepdims=True) + EPS) * g.reshape(M_HEADS, M_HD).astype(jnp.float32)
    return (h.reshape(bsz, n, M_W) * jax.nn.sigmoid(o.astype(jnp.float32))).astype(o.dtype)

def second_inputs(seed: int = 0) -> dict:
    key = jax.random.key(seed)
    ks = jax.random.split(key, 24)
    nrm = lambda k, shape, s: jax.random.normal(k, shape, jnp.float32) * s
    f_base = jnp.linspace(3.0, 6.0, M_HEADS, dtype=jnp.float32)
    return {
        'x': nrm(ks[0], (BATCH, SEQ, D_MODEL), 1.0),
        'c': nrm(ks[1], (BATCH, D_MODEL), 1.0),
        'ctx': nrm(ks[2], (BATCH, CTX_LEN, D_MODEL), 1.0),
        'c_ctx': nrm(ks[3], (D_MODEL,), 1.0),
        'w_mod': nrm(ks[4], (DEPTH, D_MODEL, N_MOD * D_MODEL), D_MODEL ** -0.5),
        'b_mod': nrm(ks[5], (DEPTH, N_MOD * D_MODEL), 0.02),
        'norm_pre': 1.0 + nrm(ks[6], (DEPTH, 3, D_MODEL), 0.05),
        'norm_post': 1.0 + nrm(ks[7], (DEPTH, 3, D_MODEL), 0.05),
        'ffn_w_in': nrm(ks[8], (DEPTH, 2, D_MODEL, 2 * D_FF_2), D_MODEL ** -0.5),
        'ffn_w_out': nrm(ks[9], (DEPTH, 2, D_FF_2, D_MODEL), D_FF_2 ** -0.5),
        'w_in': nrm(ks[10], (DEPTH, D_MODEL, IN_COLS), D_MODEL ** -0.5),
        'w_out': nrm(ks[11], (DEPTH, MIX_W, D_MODEL), MIX_W ** -0.5),
        'conv_w': nrm(ks[12], (DEPTH, CONV_W, M_W), CONV_W ** -0.5),
        'conv_b': nrm(ks[13], (DEPTH, M_W), 0.02),
        'w_q': nrm(ks[14], (DEPTH, M_HEADS, M_HD, M_HD), M_HD ** -0.5),
        'w_k': nrm(ks[15], (DEPTH, M_HEADS, M_HD, M_HD), M_HD ** -0.5),
        'i_bias': nrm(ks[16], (DEPTH, 2, M_HEADS), 0.1),
        'f_bias': f_base + nrm(ks[17], (DEPTH, 2, M_HEADS), 0.1),
        'head_norm': 1.0 + nrm(ks[18], (DEPTH, M_W), 0.05),
        'pool_w': nrm(ks[19], (DEPTH, POOL_GROUPS, POOL_GW, POOL_GW), POOL_GW ** -0.5),
        'pool_scale': 1.0 + nrm(ks[20], (DEPTH, POOL_W), 0.1),
    }

def second_block(x, c, ctx, c_ctx, w_mod, b_mod, norm_pre, norm_post, ffn_w_in, ffn_w_out, w_in, w_out,
              conv_w, conv_b, w_q, w_k, i_bias, f_bias, head_norm, pool_w, pool_scale):
    sc = jax.nn.silu(c)
    scc = jax.nn.silu(c_ctx)[None]
    xc = ctx
    for l in range(DEPTH):
        ctx_out = l < DEPTH - 1
        mod = (sc @ w_mod[l] + b_mod[l]).reshape(-1, N_MOD, D_MODEL)
        modc = (scc @ w_mod[l] + b_mod[l]).reshape(1, N_MOD, D_MODEL)
        x = ada_out(x, swiglu(ada_in(x, mod, 0, norm_pre[l, 0]), ffn_w_in[l, 0], ffn_w_out[l, 0]),
                    mod, 0, norm_post[l, 0], 0.5)
        xc = ada_out(xc, swiglu(ada_in(xc, modc, 0, norm_pre[l, 0]), ffn_w_in[l, 0], ffn_w_out[l, 0]),
                     modc, 0, norm_post[l, 0], 0.5)
        p = ada_in(x, mod, 1, norm_pre[l, 1]) @ w_in[l]
        pc = ada_in(xc, modc, 1, norm_pre[l, 1]) @ (w_in[l] if ctx_out else w_in[l, :, :M_COLS])
        h_lat, h_ctx = mlstm_bidir(p[..., :M_COLS], pc[..., :M_COLS], conv_w[l], conv_b[l],
                                   w_q[l], w_k[l], i_bias[l], f_bias[l])
        mix = jnp.concatenate([mlstm_out(h_lat, p[..., 2 * M_W:3 * M_W], head_norm[l]),
                               pool_mixer(p[..., M_COLS:], pool_w[l], pool_scale[l], True)], axis=-1)
        x = ada_out(x, mix @ w_out[l], mod, 1, norm_post[l, 1], 1.0)
        if ctx_out:
            mixc = jnp.concatenate([mlstm_out(h_ctx, pc[..., 2 * M_W:3 * M_W], head_norm[l]),
                                    pool_mixer(pc[..., M_COLS:], pool_w[l], pool_scale[l], False)], axis=-1)
            xc = ada_out(xc, mixc @ w_out[l], modc, 1, norm_post[l, 1], 1.0)
        x = ada_out(x, swiglu(ada_in(x, mod, 2, norm_pre[l, 2]), ffn_w_in[l, 1], ffn_w_out[l, 1]),
                    mod, 2, norm_post[l, 2], 0.5)
        if ctx_out:
            xc = ada_out(xc, swiglu(ada_in(xc, modc, 2, norm_pre[l, 2]), ffn_w_in[l, 1], ffn_w_out[l, 1]),
                         modc, 2, norm_post[l, 2], 0.5)
    return x


def setup_inputs(seed=0):
    out = dict(first_inputs(seed))
    for name, value in second_inputs(seed + 1).items():
        if name != "x":
            out[name + "_2"] = value
    return out


def reference(
    x, c, w_ada, b_ada, g_pre_mix, g_post_mix, g_pre_ffn, g_post_ffn, w_in, cmp_pe, cmp_w1,
    cmp_b1, cmp_w2, cmp_b2, g_kv_norm, w_uk, w_uv, w_out, w_gate_up, w_down, c_2, ctx_2,
    c_ctx_2, w_mod_2, b_mod_2, norm_pre_2, norm_post_2, ffn_w_in_2, ffn_w_out_2, w_in_2,
    w_out_2, conv_w_2, conv_b_2, w_q_2, w_k_2, i_bias_2, f_bias_2, head_norm_2, pool_w_2,
    pool_scale_2,
):
    x = first_block(
        x, c, w_ada, b_ada, g_pre_mix, g_post_mix, g_pre_ffn, g_post_ffn, w_in, cmp_pe, cmp_w1,
        cmp_b1, cmp_w2, cmp_b2, g_kv_norm, w_uk, w_uv, w_out, w_gate_up, w_down,
    )
    return second_block(
        x, c_2, ctx_2, c_ctx_2, w_mod_2, b_mod_2, norm_pre_2, norm_post_2, ffn_w_in_2,
        ffn_w_out_2, w_in_2, w_out_2, conv_w_2, conv_b_2, w_q_2, w_k_2, i_bias_2, f_bias_2,
        head_norm_2, pool_w_2, pool_scale_2,
    )


_drawn_inputs = setup_inputs


def setup_inputs(seed=0):
    import zlib

    import numpy as np

    out = dict(_drawn_inputs(seed))
    spreads = {}
    factors = {'g_post_mix': 2.681,
     'g_post_ffn': 3.366,
     'cmp_b1': 49.474,
     'cmp_b2': 24.174,
     'g_kv_norm': 3.978,
     'conv_b_2': 4.337,
     'i_bias_2': 8.0,
     'head_norm_2': 18.969,
     'cmp_pe': 5.314,
     'pool_scale_2': 4.537}
    for name, (base, spread) in spreads.items():
        noise = np.random.default_rng([zlib.crc32(name.encode()), seed]).standard_normal(out[name].shape)
        drawn = base * np.exp(spread * noise) if base else spread * noise
        out[name] = __import__('jax').numpy.asarray(drawn.astype(out[name].dtype))
    for name, factor in factors.items():
        out[name] = (out[name] * factor).astype(out[name].dtype)
    return out
```

```python
from contextlib import ExitStack

import numpy as np

import concourse.bass as bass
from concourse import mybir

F32 = mybir.dt.float32
ALU = mybir.AluOpType
ACT = mybir.ActivationFunctionType
AX = mybir.AxisListType

P = 128
D = 1024
KT = D // P
SEQ = 512
CTX = 256
TOK = CTX + SEQ
QT = SEQ // P
HD = 64
ROPE = HD // 4
HEADS = 8
NCMP = (SEQ - 32) // 16 + 1
TOPK = 128
FF = 2816
FT = FF // P
MH = 4
CH = TOK // P
CC = CTX // P
NEG = -1e30
EPS = 1e-6
SCALE = HD ** -0.5
UNSEEN = -3.0e38
TAKEN = -3.4e38

CONST = {}
_at = 0
for _name, _n in (("ident", P), ("rot", P), ("esel", P), ("cos", SEQ), ("sin", SEQ), ("causal", SEQ),
                  ("cmp_add", QT * NCMP), ("cmp_one", QT * NCMP), ("tri_f", P), ("tri_b", P)):
    CONST[_name] = (_at, _at + _n)
    _at += _n
NCONST = _at

ROWS_A = [("b_ada", 48), ("g_pre_mix", 8), ("g_post_mix", 8), ("g_pre_ffn", 8), ("g_post_ffn", 8),
          ("c", 8), ("c_2", 8), ("c_ctx_2", 8)]
ROWS_B = [("b_mod_2", 72), ("norm_pre_2", 24), ("norm_post_2", 24)]
ROWS_C = [("conv_w_2", 12), ("conv_b_2", 4), ("head_norm_2", 4), ("pool_scale_2", 4), ("cmp_b1", 2),
          ("cmp_b2", 1), ("cmp_pe", 32)]
PCOL = {}
for _g, _rows in enumerate((ROWS_A, ROWS_B, ROWS_C)):
    _r = 0
    for _name, _n in _rows:
        PCOL[_name] = (_g, _r, _n)
        _r += _n
    PCOL[_g] = _r

IN1 = {}
_at = 0
for _name, _n in (("nq", 512), ("nkc", 128), ("nvc", 128), ("nks", 128), ("nvs", 128), ("nkw", 128), ("nvw", 128),
                  ("gate", 24), ("dq", 512), ("dckv", 128), ("dkr", 16), ("iq", 512), ("ik", 64), ("iw", 8)):
    IN1[_name] = (_at, _at + _n)
    _at += _n
ROWC = {"nvs": (0, 128), "nvw": (128, 256), "gate": (256, 280), "dckv": (280, 408), "iw": (408, 416)}
NROWC = 416
M_U, M_V, M_O, M_G, M_POOL = 0, 512, 1024, 1536, 1552

RING = 3
RW = 4096


class Fields:
    pass


class Steps:

    def __init__(self, sem):
        self.sem, self.n = sem, 0

    def link(self, eng, ins):
        self.n += 1
        ins.then_inc(self.sem, 1)
        eng.wait_ge(self.sem, self.n)


class Tally:

    def __init__(self, sem):
        self.sem, self.base = sem, 0

    def wait(self, eng, n):
        eng.wait_ge(self.sem, self.base + n)

    def close(self, n):
        self.base += n


def weight_items(A):
    items = {}

    def cols(w, a, b):
        return w.rearrange("(k p) n -> p k n", p=P)[:, :, a:b]

    def block(name, w, a, b, width=None):
        n = b - a
        items[name] = [(lambda r, n=n: r[:, 0:KT * n].rearrange("p (k n) -> p k n", k=KT), cols(w, a, b))]

    def view(width, a, b):
        return lambda r: r[:, 0:KT * width].rearrange("p (k n) -> p k n", k=KT)[:, :, a:b]

    ada, mod, win = A["w_ada"][0], A["w_mod_2"][0], A["w_in"][0]

    def modulations(kind, *numbers):
        for i in numbers:
            block((kind, i), ada if kind == "ada" else mod, 512 * i, 512 * i + 512)

    for n in range(4):
        block(("ada", n), ada, 512 * n, 512 * n + 512)
    items["nq"] = [(view(512, 128 * j + 64 * g, 128 * j + 64 * g + 64), cols(win, 256 * g + 64 * j, 256 * g + 64 * j + 64))
                   for j in range(4) for g in range(2)]
    modulations("ada", 4)
    items["kv"] = [(view(512, 0, 384), cols(win, IN1["nkc"][0], IN1["nks"][1])),
                   (view(512, 384, 512), cols(win, *IN1["nkw"]))]
    modulations("ada", 5)
    items["rows"] = [(view(NROWC, *ROWC["nvs"]), cols(win, *IN1["nvs"])),
                     (view(NROWC, ROWC["nvw"][0], ROWC["gate"][1]), cols(win, IN1["nvw"][0], IN1["gate"][1])),
                     (view(NROWC, *ROWC["dckv"]), cols(win, *IN1["dckv"])),
                     (view(NROWC, *ROWC["iw"]), cols(win, *IN1["iw"]))]
    modulations("ada", 6)
    block("dq", win, *IN1["dq"])
    modulations("ada", 7)
    block("iq", win, *IN1["iq"])
    modulations("ada", 8)
    items["small"] = [(view(144, 0, 16), cols(win, *IN1["dkr"]))]
    items["small"] += [(view(144, 16 + 64 * i, 80 + 64 * i), cols(win, *IN1["ik"])) for i in range(2)]
    modulations("ada", 9, 10, 11)
    items["cmp"] = [(lambda r, i=i: r[:, 2048 * i:2048 * i + 2048].rearrange("p (m h) -> p m h", m=16),
                     A["cmp_w1"][0, i].rearrange("(m p) h -> p m h", p=P)) for i in range(2)]
    for half in range(2):
        a, b = 512 * half, 512 * half + 512
        wo = A["w_out"][0]
        items[("out1", half)] = [
            (lambda r: r[0:64, :].rearrange("p (k n) -> p k n", k=KT)[:, 0:4],
             wo[0:256].rearrange("(j p) n -> p j n", p=64)[:, :, a:b]),
            (lambda r: r[64:128, :].rearrange("p (k n) -> p k n", k=KT)[:, 0:4],
             wo[256:512].rearrange("(j p) n -> p j n", p=64)[:, :, a:b]),
            (lambda r: r[:, :].rearrange("p (k n) -> p k n", k=KT)[:, 4:8],
             wo[512:1024].rearrange("(j p) n -> p j n", p=P)[:, :, a:b])]

    def ffn(n, wi, wo):
        rest = list(range(18)) if n == 0 else []
        for g in range(FT // 2):
            items[("up", n, g)] = [
                (lambda r, h=h: r[:, :].rearrange("p (k h n) -> p k h n", k=KT, h=2)[:, :, h],
                 cols(wi, FF * h + 256 * g, FF * h + 256 * g + 256)) for h in range(2)]
            modulations("mod", *rest[g:g + 1])
        for half in range(2):
            for s in range(3):
                f0, f1 = 8 * s, min(8 * s + 8, FT)
                items[("down", n, half, s)] = [
                    (lambda r, m=f1 - f0: r[:, 0:512 * m].rearrange("p (f n) -> p f n", n=512),
                     wo[f0 * P:f1 * P].rearrange("(f p) n -> p f n", p=P)[:, :, 512 * half:512 * half + 512])]
                first = 11 + 3 * half + s + (s + half > 0)
                modulations("mod", *rest[first:first + (2 if s + half == 0 else 1)])

    ffn(0, A["w_gate_up"][0], A["w_down"][0])
    ffn(1, A["ffn_w_in_2"][0, 0], A["ffn_w_out_2"][0, 0])
    for name, a in (("u", M_U), ("v", M_V), ("o", M_O), ("pool", M_POOL)):
        block(name, A["w_in_2"][0], a, a + 512)
    block(("out2", 0), A["w_out_2"][0], 0, 512)
    block(("out2", 1), A["w_out_2"][0], 512, 1024)
    ffn(2, A["ffn_w_in_2"][0, 1], A["ffn_w_out_2"][0, 1])
    return items


class Ring:

    def __init__(self, nc, A, buf):
        self.buf = buf
        self.items = list(weight_items(A).items())
        self.place = {name: i for i, (name, _) in enumerate(self.items)}
        self.filled = [nc.alloc_semaphore(f"ring_filled{i}") for i in range(RING)]
        self.freed = nc.alloc_semaphore("ring_freed")
        self.loaded = 0
        self.used = 0
        self.n_freed = 0
        self.leaves = {}
        self.due, count = [], [0] * RING
        for i, (_, parts) in enumerate(self.items):
            count[i % RING] += 16 * len(parts)
            self.due.append(count[i % RING])

    def load_ahead(self, sp):
        end = min(self.used + RING, len(self.items))
        while self.loaded < end:
            i = self.loaded
            if i >= RING:
                sp.wait_ge(*self.leaves[i - RING])
            for dst, src in self.items[i][1]:
                sp.dma_start(dst(self.buf[:, i % RING, :]), src).then_inc(self.filled[i % RING], 16)
            self.loaded += 1

    def take(self, eng, name):
        i = self.place[name]
        self.current = i
        self.used = max(self.used, i + 1)
        eng.wait_ge(self.filled[i % RING], self.due[i])
        return self.buf[:, i % RING, :]

    def left(self, sem, value):
        self.leaves[self.current] = (sem, value)

    def free(self, last):
        self.n_freed += 1
        last.then_inc(self.freed, 1)
        self.left(self.freed, self.n_freed)


def build(nc, A, out):
    K = Fields()
    with ExitStack() as ctx:
        def sb(name, shape, stack=ctx):
            return stack.enter_context(nc.sbuf_tensor(name, shape, F32))

        K.nc, K.A = nc, A
        K.ps = [ctx.enter_context(nc.psum_tensor(f"ps{i}", [P, 512], F32)) for i in range(8)]
        K.ring = Ring(nc, A, sb("ring", [P, RING, RW]))
        K.x = sb("x_res", [P, KT, TOK])
        K.h = sb("h_act", [P, KT, TOK])
        K.cst = sb("cst", [P, NCONST])
        K.ones = sb("ones", [P, P])
        K.eps = sb("eps", [P, 1])
        K.par = [sb(f"par{g}", [P, PCOL[g]]) for g in range(3)]
        K.cc1 = sb("cc1", [P, KT])
        K.cc2 = sb("cc2", [P, KT, 2])
        K.mod1 = sb("mod1", [P, 48])
        K.mod2 = sb("mod2", [P, 72, 2])
        K.coef = sb("coef", [P, 12, KT])
        K.sq = sb("sq", [P, 2, 512])
        K.tmp = sb("tmp", [P, 2, 512])
        K.rstd = sb("rstd", [P, 2, 512])
        K.act = Steps(nc.alloc_semaphore("act_step"))
        K.dve = Steps(nc.alloc_semaphore("dve_step"))
        K.pool = Steps(nc.alloc_semaphore("pool_step"))
        K.sem = nc.alloc_semaphore
        K.sb = sb
        K.mod_sum, K.mod_mm = nc.alloc_semaphore("mod_sum"), nc.alloc_semaphore("mod_mm")
        K.mods_summed = K.mods_turned = 0
        K.norm_sems = {n: Tally(nc.alloc_semaphore(f"norm_{n}")) for n in ("sq", "mm", "std", "tmp", "out")}
        K.ffn_sems = {n: Tally(nc.alloc_semaphore(f"ffn_{n}"))
                      for n in ("up_mm", "silu", "hid", "down_mm", "down_out")}
        K.c = lambda name: K.cst[:, CONST[name][0]:CONST[name][1]]

        def par(name, i=0, n=None):
            g, r, m = PCOL[name]
            return K.par[g][:, r + i:r + (m if n is None else i + n)]
        K.p = par

        stages = [stage_start, stage_mixer_1, stage_ffn_1, stage_ffn_2, stage_mixer_2, stage_ffn_3, stage_end]
        for stage in stages:
            stage(K, out)


def const(K, name, rows=P):
    a, b = CONST[name]
    return K.cst[0:rows, a:b]


def stage_start(K, out):
    nc, A = K.nc, K.A
    const_in, param_in, x_in = K.sem("const_in"), K.sem("param_in"), K.sem("x_in")
    set_done, par_t, par_done = K.sem("set_done"), K.sem("par_t"), K.sem("par_done")
    turned, kept, silu_done = K.sem("x_turned"), K.sem("x_kept"), K.sem("silu_done")
    with ExitStack() as st:
        xr = K.sb("x_rows", [P, QT, D], st)
        cr = K.sb("ctx_rows", [P, CC, D], st)
        prow = K.sb("param_rows", [P, 3, P], st)
        with nc.Block() as block:

            n_params = 0

            @block.vector
            def _(dve):
                dve.memset(K.ones[:, :], 1.0)
                dve.memset(K.eps[:, :], EPS).then_inc(set_done, 1)
                for g in range(3):
                    dve.wait_ge(par_t, g + 1)
                    dve.tensor_copy(K.par[g][:, :], K.ps[g][:, 0:PCOL[g]]).then_inc(par_done, 1)
                for k in range(0, KT):
                    for part in range(2):
                        i = 2 * k + part
                        dve.wait_ge(turned, i + 1)
                        dst = K.x[:, k, CTX:TOK] if part == 0 else K.x[:, k, 0:CTX]
                        src = K.ps[3 + i % 4][:, 0:SEQ if part == 0 else CTX]
                        dve.tensor_copy(dst, src).then_inc(kept, 1)
                dve.wait_ge(silu_done, 1)
                for n in range(4):
                    modulation_sums(K, dve, ("ada", n))
                dve.wait_ge(K.mod_mm, 4)
                dve.tensor_tensor(K.mod1[:, 0:16], K.ps[7][:, 0:16], K.p("b_ada", 0, 16), ALU.add).then_inc(kept, 1)
                dve.wait_ge(kept, 2 * KT + 1)
                dve.scalar_tensor_tensor(K.coef[:, 0], K.mod1[:, 8:16], 1.0, K.p("g_pre_mix"), ALU.add,
                                         ALU.mult).then_inc(kept, 1)

            @block.scalar
            def _(act):
                nonlocal n_params

                def row(name, src):
                    nonlocal n_params
                    g, r, n = PCOL[name]
                    act.dma_start(prow[r:r + n, g, :], src).then_inc(param_in, 16)
                    n_params += 1
                row("b_ada", A["b_ada"][0].rearrange("(r p) -> r p", p=P))
                for name in ("g_pre_mix", "g_post_mix", "g_pre_ffn", "g_post_ffn", "c"):
                    row(name, A[name][0].rearrange("(r p) -> r p", p=P))
                row("c_2", A["c_2"][0].rearrange("(r p) -> r p", p=P))
                row("c_ctx_2", A["c_ctx_2"].rearrange("(r p) -> r p", p=P))
                row("b_mod_2", A["b_mod_2"][0].rearrange("(r p) -> r p", p=P))
                row("norm_pre_2", A["norm_pre_2"][0].rearrange("j (r p) -> (j r) p", p=P))
                row("norm_post_2", A["norm_post_2"][0].rearrange("j (r p) -> (j r) p", p=P))
                row("conv_w_2", A["conv_w_2"][0].rearrange("j (r p) -> (j r) p", p=P))
                row("conv_b_2", A["conv_b_2"][0].rearrange("(r p) -> r p", p=P))
                row("head_norm_2", A["head_norm_2"][0].rearrange("(r p) -> r p", p=P))
                row("pool_scale_2", A["pool_scale_2"][0].rearrange("(r p) -> r p", p=P))
                row("cmp_b1", A["cmp_b1"][0])
                row("cmp_pe", A["cmp_pe"][0].rearrange("i (m e) d -> (i m) (e d)", e=2))
                g, r, _n = PCOL["cmp_b2"]
                for half in range(2):
                    act.dma_start(prow[r:r + 1, g, 64 * half:64 * half + 64], A["cmp_b2"][0, 0:1]).then_inc(param_in, 16)
                    n_params += 1
                act.wait_ge(par_done, 1)
                act.activation(K.cc1[:, :], K.p("c"), ACT.Silu)
                act.activation(K.cc2[:, :, 0], K.p("c_2"), ACT.Silu)
                act.activation(K.cc2[:, :, 1], K.p("c_ctx_2"), ACT.Silu).then_inc(silu_done, 1)

            @block.tensor
            def _(pe):
                pe.wait_ge(const_in, 16)
                pe.wait_ge(param_in, 16 * n_params)
                for g in range(3):
                    n = PCOL[g]
                    pe.transpose(K.ps[g][:, 0:n], prow[0:n, g, :], const(K, "ident")[0:n, 0:n]).then_inc(par_t, 1)
                pe.wait_ge(x_in, 32)
                for k in range(KT):
                    for part in range(2):
                        i = 2 * k + part
                        if i >= 4:
                            pe.wait_ge(kept, i - 3)
                        src = xr if part == 0 else cr
                        for t in range(QT if part == 0 else CC):
                            last = pe.transpose(K.ps[3 + i % 4][:, t * P:t * P + P], src[:, t, k * P:k * P + P],
                                                const(K, "ident"))
                        last.then_inc(turned, 1)
                for n in range(4):
                    modulation_columns(K, pe, ("ada", n))

            @block.sync
            def _(sp):
                sp.dma_start(K.cst[:, :], A["consts"]).then_inc(const_in, 16)
                sp.dma_start(xr[:, :, :], A["x"][0].rearrange("(t p) d -> p t d", p=P)).then_inc(x_in, 16)
                sp.dma_start(cr[:, :, :], A["ctx_2"][0].rearrange("(t p) d -> p t d", p=P)).then_inc(x_in, 16)
                K.ring.load_ahead(sp)


def modulation_sums(K, dve, name):
    kind, n = name
    w = K.ring.take(dve, name).rearrange("p (k n) -> p k n", k=KT)
    m = K.mods_summed
    vecs = [K.cc1[:, :]] if kind == "ada" else [K.cc2[:, :, v] for v in range(2)]
    if m >= 2:
        dve.wait_ge(K.mod_mm, m - 1)
    for k in range(KT):
        if k:
            dve.wait_ge(K.dve.sem, K.dve.n)
        for v, c in enumerate(vecs):
            acc = (K.sq, K.tmp)[v][:, m % 2, :]
            if k == 0:
                ins = dve.tensor_scalar(acc, w[:, k, :], c[:, k:k + 1], None, ALU.mult)
            else:
                ins = dve.scalar_tensor_tensor(acc, w[:, k, :], c[:, k:k + 1], acc, ALU.mult, ALU.add)
            if v == len(vecs) - 1:
                if k == KT - 1:
                    ins.then_inc(K.mod_sum, 1)
                else:
                    K.dve.n += 1
                    ins.then_inc(K.dve.sem, 1)
    K.mods_summed += 1
    K.ring.left(K.mod_sum, K.mods_summed)


def modulation_columns(K, pe, name):
    kind, n = name
    m = K.mods_turned
    pe.wait_ge(K.mod_sum, m + 1)
    for c in range(4):
        j = 4 * n + c
        for v in range(1 if kind == "ada" else 2):
            col = j if kind == "ada" else 48 + 2 * j + v
            last = pe.matmul(K.ps[7][:, col:col + 1], (K.sq, K.tmp)[v][:, m % 2, c * P:c * P + P], K.ones[:, 0:1],
                             start=True, stop=True)
    last.then_inc(K.mod_mm, 1)
    K.mods_turned += 1


def norm_in(src, n, scale, shift, dst, after=False):
    return dict(src=src, n=n, scale=scale, shift=shift, dst=dst, after=after)


def norm_out(src, n, gain, res):
    return dict(src=src, n=n, gain=gain, dst=None, res=res, after=False)


def rms_norms(K, jobs):
    nc, S = K.nc, K.norm_sems
    back = (len(jobs) + 1) // 2
    with nc.Block() as block:

        @block.scalar
        def _(act):
            for j, job in enumerate(jobs):
                n = job["n"]
                for k in range(KT):
                    i = KT * j + k
                    if i >= 2:
                        S["mm"].wait(act, i - 1)
                    if job["after"]:
                        S["out"].wait(act, KT * (j - back) + k + 1)
                    act.activation(K.sq[:, i % 2, 0:n], job["src"](k), ACT.Square).then_inc(S["sq"].sem, 1)
                S["mm"].wait(act, KT * (j + 1))
                if j >= 2:
                    S["out"].wait(act, KT * (j - 1))
                act.activation(K.rstd[:, j % 2, 0:n], K.ps[j][:, 0:n], ACT.Sqrt, bias=K.eps[:, 0:1],
                               scale=1.0 / D).then_inc(S["std"].sem, 1)
            for j, job in enumerate(jobs):
                if job["dst"] is not None:
                    for k in range(KT):
                        i = KT * j + k
                        S["tmp"].wait(act, i + 1)
                        act.activation(job["dst"](k), K.tmp[:, i % 2, 0:job["n"]], ACT.Identity,
                                       bias=job["shift"][:, k:k + 1],
                                       scale=job["scale"][:, k:k + 1]).then_inc(S["out"].sem, 1)

        @block.tensor
        def _(pe):
            for j, job in enumerate(jobs):
                n = job["n"]
                for k in range(KT):
                    i = KT * j + k
                    S["sq"].wait(pe, i + 1)
                    pe.matmul(K.ps[j][:, 0:n], K.ones[:, :], K.sq[:, i % 2, 0:n], start=(k == 0),
                              stop=(k == KT - 1)).then_inc(S["mm"].sem, 1)

        @block.vector
        def _(dve):
            for j, job in enumerate(jobs):
                n = job["n"]
                rstd = K.rstd[:, j % 2, 0:n]

                def add(k):
                    i = KT * j + k
                    S["tmp"].wait(dve, i + 1)
                    dve.scalar_tensor_tensor(job["res"](k), K.tmp[:, i % 2, 0:n], job["gain"][:, k:k + 1],
                                             job["res"](k), ALU.mult, ALU.add).then_inc(S["out"].sem, 1)
                S["std"].wait(dve, j + 1)
                K.dve.link(dve, dve.reciprocal(rstd, rstd))
                for k in range(KT):
                    i = KT * j + k
                    if i >= 2:
                        S["out"].wait(dve, i - 1)
                    dve.tensor_tensor(K.tmp[:, i % 2, 0:n], job["src"](k), rstd, ALU.mult).then_inc(S["tmp"].sem, 1)
                    if job["dst"] is None and k:
                        add(k - 1)
                if job["dst"] is None:
                    add(KT - 1)

    for name in ("sq", "mm", "tmp", "out"):
        S[name].close(KT * len(jobs))
    S["std"].close(len(jobs))


def lat(t):
    return lambda k: t[:, k, CTX:TOK]


def ctxt(t):
    return lambda k: t[:, k, 0:CTX]


def stage_mixer_1(K, out):
    rms_norms(K, [norm_in(lat(K.x), SEQ, K.coef[:, 0], K.mod1[:, 0:8], lat(K.h))])
    with ExitStack() as st:
        M = Fields()
        M.q = K.sb("q_t", [P, 4, SEQ], st)
        M.kv = K.sb("kv_t", [P, 4, SEQ], st)
        M.dq = K.sb("dq_t", [P, 4, SEQ], st)
        M.rows = K.sb("row_cols", [P, QT, NROWC], st)
        M.cT = K.sb("latent_t", [P, SEQ], st)
        M.kd = K.sb("dsa_k", [P, 4, SEQ], st)
        M.vd = K.sb("dsa_v", [P, QT, SEQ], st)
        M.sel = K.sb("picked", [P, QT, SEQ], st)
        M.kc = K.sb("kc_t", [P, NCMP], st)
        M.vc = K.sb("vc_rows", [NCMP, 2, HD], st)
        M.b2v = K.sb("b2_rows", [NCMP, HD], st)
        M.gkv = K.sb("gkv_rows", [P, P], st)
        M.wuk = K.sb("w_uk", [P, HEADS, HD], st)
        M.wuv = K.sb("w_uv", [P, HEADS, HD], st)
        M.kr = K.sb("kr_t", [ROPE, SEQ], st)
        M.small_in = K.sem("m1_small_in")
        with ExitStack() as st2:
            M.iq = K.sb("iq_t", [P, 4, SEQ], st2)
            M.ik = K.sb("ik_t", [P, SEQ], st2)
            M.raw = K.sb("raw_t", [P, 3, SEQ], st2)
            M.kk = K.h[:, 0:4, CTX:TOK].rearrange("p (i g) n -> p i g n", i=2)
            M.hid = K.sb("cmp_hid", [P, 2, 2 * NCMP], st2)
            M.bias = K.sb("cmp_bias", [P, 2], st2)
            M.ss = K.sb("ckv_ss", [P, 2, QT], st2)
            M.rsc = K.sq
            M.score = M.raw[:, 0, :]
            M.top = K.sb("idx_top", [P, 8], st2)
            project_1(K, M)
            latent_and_compressed(K, M)
            indexer(K, M)
        M.pct = K.sb("cmp_pt", [NCMP, QT, HEADS, P], st)
        M.pc = K.sb("cmp_p", [P, 2, HEADS, NCMP], st)
        M.pcs = K.sb("cmp_stat", [P, 2, HEADS], st)
        compressed_probs(K, M)
        M.p = [K.sq[:, 0, :], K.sq[:, 1, :], K.sb("probs", [P, SEQ], st)]
        M.pt = K.tmp
        M.stat = K.sb("soft_stat", [P, 3, 4], st)
        attention(K, M)
    with ExitStack() as st:
        y = K.sb("mix_out", [P, KT, SEQ], st)
        coefs_1(K)
        project_out(K, "out1", y, 0)
        rms_norms(K, [norm_out(lambda k: y[:, k, :], SEQ, K.coef[:, 1], lat(K.x)),
                      norm_in(lat(K.x), SEQ, K.coef[:, 2], K.mod1[:, 24:32], lat(K.h), after=True)])


def project_1(K, M):
    nc, A = K.nc, K.A
    mm, rawd, rotd, roped, rowd, rowk = (K.sem(f"p1_{n}") for n in ("mm", "raw", "rot", "rope", "rowmm", "row"))
    tiles = [("nq", j, M.q[:, j, :], P, True) for j in range(4)]
    tiles += [("kv", j, M.kv[:, j, :], P, j != 1) for j in range(4)]
    tiles += [("rows", 0, None, P, False)]
    tiles += [("dq", j, M.dq[:, j, :], P, True) for j in range(4)]
    tiles += [("iq", j, M.iq[:, j, :], P, True) for j in range(4)]
    tiles += [("small", 0, M.kr[:, :], ROPE, True), ("small", 1, M.ik[:, :], P, True)]
    t_tiles = [t for t in tiles if t[0] != "rows"]
    after = {"nq": (4,), "kv": (5,), "rows": (6,), "dq": (7,), "iq": (8,), "small": (9, 10, 11)}
    turns = {"kv": "nq", "rows": "kv", "dq": "rows", "iq": "dq", "small": "iq"}
    hl = lat(K.h)

    def lhs(w, item, j, k):
        if item == "small":
            v = w[:, 0:KT * 144].rearrange("p (k n) -> p k n", k=KT)
            return v[:, k, 0:16] if j == 0 else v[:, k, 16:144]
        return w[:, 0:KT * 512].rearrange("p (k n) -> p k n", k=KT)[:, k, j * P:j * P + P]

    with nc.Block() as block:

        @block.tensor
        def _(pe):
            def rotate(i):
                item, j, dst, rows, rope = t_tiles[i]
                if rope:
                    n = sum(t[4] for t in t_tiles[:i])
                    pe.wait_ge(rawd, i + 1)
                    if n >= 2:
                        pe.wait_ge(roped, n - 1)
                    pe.matmul(K.ps[3 + n % 2][0:rows, :], const(K, "rot")[0:rows, 0:rows], M.raw[0:rows, i % 3, :],
                              start=True, stop=True).then_inc(rotd, 1)

            i = 0
            for item, group in (("nq", 4), ("kv", 4), ("rows", 1), ("dq", 4), ("iq", 4), ("small", 2)):
                w = K.ring.take(pe, item)
                if item == "rows":
                    rotate(i - 1)
                    for t in range(QT):
                        if t >= 2:
                            pe.wait_ge(rowk, 1 + t - 1)
                        wv = w[:, 0:KT * NROWC].rearrange("p (k n) -> p k n", k=KT)
                        for k in range(KT):
                            last = pe.matmul(K.ps[5 + t % 2][:, 0:NROWC], K.h[:, k, CTX + t * P:CTX + t * P + P],
                                             wv[:, k, :], start=(k == 0), stop=(k == KT - 1))
                        last.then_inc(rowd, 1)
                    K.ring.left(rowd, QT)
                else:
                    for j in range(group):
                        rows = t_tiles[i][3]
                        if i >= 3:
                            pe.wait_ge(rawd, i - 2)
                        for k in range(KT):
                            last = pe.matmul(K.ps[i % 3][0:rows, :], lhs(w, item, j, k), hl(k), start=(k == 0),
                                             stop=(k == KT - 1))
                        last.then_inc(mm, 1)
                        if j == group - 1:
                            K.ring.left(mm, i + 1)
                        if i >= 1 and i != 8:
                            rotate(i - 1)
                        i += 1
                for n in after[turns[item]] if item in turns else ():
                    modulation_columns(K, pe, ("ada", n))
            rotate(i - 1)
            for n in after["small"]:
                modulation_columns(K, pe, ("ada", n))

        @block.scalar
        def _(act):
            n = 0
            for i, (item, j, dst, rows, rope) in enumerate(t_tiles):
                act.wait_ge(mm, i + 1)
                if rope and i >= 3:
                    act.wait_ge(roped, sum(t[4] for t in t_tiles[:i - 2]))
                act.activation(M.raw[0:rows, i % 3, :] if rope else dst, K.ps[i % 3][0:rows, :],
                               ACT.Copy).then_inc(rawd, 1)

        @block.vector
        def _(dve):
            dve.memset(M.wuk[:, :, :], 0.0).then_inc(rowk, 1)
            n = 0
            for i, (item, j, dst, rows, rope) in enumerate(t_tiles):
                if i == 8:
                    for t in range(QT):
                        dve.wait_ge(rowd, t + 1)
                        dve.tensor_copy(M.rows[:, t, :], K.ps[5 + t % 2][:, 0:NROWC]).then_inc(rowk, 1)
                    for m in after["rows"]:
                        modulation_sums(K, dve, ("ada", m))
                if rope:
                    raw = M.raw[0:rows, i % 3, :]
                    dve.wait_ge(rotd, n + 1)
                    K.dve.link(dve, dve.tensor_tensor(K.tmp[0:rows, n % 2, :], K.ps[3 + n % 2][0:rows, :],
                                                      const(K, "sin")[0:rows, :], ALU.mult))
                    K.dve.link(dve, dve.tensor_tensor(dst, raw, const(K, "cos")[0:rows, :], ALU.mult))
                    dve.tensor_tensor(dst, dst, K.tmp[0:rows, n % 2, :], ALU.add).then_inc(roped, 1)
                    n += 1
                ends = {3: "nq", 7: "kv", 11: "dq", 15: "iq", 17: "small"}
                for m in after[ends[i]] if i in ends else ():
                    modulation_sums(K, dve, ("ada", m))

        @block.sync
        def _(sp):
            sp.dma_start(M.gkv[:, :], A["g_kv_norm"].broadcast_to([P, P])).then_inc(M.small_in, 16)
            sp.dma_start(M.b2v[:, :], A["cmp_b2"][0, 1:2].broadcast_to([NCMP, HD])).then_inc(M.small_in, 16)
            sp.dma_start(M.wuv[:, :, :], A["w_uv"][0].rearrange("h r d -> r h d")).then_inc(M.small_in, 16)
            sp.wait_ge(rowk, 1)
            sp.dma_start(M.wuk[:, :, ROPE:HD], A["w_uk"][0].rearrange("h r e -> r h e")).then_inc(M.small_in, 16)
            K.ring.load_ahead(sp)


def latent_and_compressed(K, M):
    nc = K.nc
    kk_in, sq, std, nrm, ct, ctk, kdm, vdm, kvk = (K.sem(f"lc_{n}") for n in (
        "kk", "sq", "std", "norm", "turn", "turned", "kmm", "vmm", "kept"))
    hidm, hidd, biasd, w2in, cmm, cmk = (K.sem(f"lc_{n}") for n in ("hidmm", "hid", "bias", "w2", "cmm", "cmk"))
    with ExitStack() as st, nc.Block() as block:
        w2 = K.sb("cmp_w2", [P, 3, HD], st)

        @block.scalar
        def _(act):
            for t in range(QT):
                act.activation(M.rsc[:, 0, t * P:t * P + P], M.rows[:, t, ROWC["dckv"][0]:ROWC["dckv"][1]], ACT.Square,
                               accum_out=M.ss[:, 0, t:t + 1]).then_inc(sq, 1)
            act.wait_ge(sq, QT)
            act.activation(M.ss[:, 1, :], M.ss[:, 0, :], ACT.Sqrt, bias=K.eps[:, 0:1], scale=1.0 / P).then_inc(std, 1)
            for t in range(QT):
                g = M.rows[:, t, ROWC["gate"][0]:ROWC["gate"][1]]
                act.activation(g, g, ACT.Sigmoid).then_inc(sq, 1)
            act.wait_ge(ct, 1)
            act.activation(M.cT[:, :], K.ps[0][:, :], ACT.Copy).then_inc(ctk, 1)
            for j in range(4):
                act.wait_ge(kdm, j + 1)
                act.activation(M.kd[:, j, :], K.ps[1 + j % 2][:, :], ACT.Copy).then_inc(kvk, 1)
            for i in range(2):
                act.wait_ge(biasd, i + 1)
                act.activation(M.hid[:, i, :], K.ps[5 + i][:, 0:2 * NCMP], ACT.Gelu_apprx_tanh,
                               bias=M.bias[:, i:i + 1]).then_inc(hidd, 1)

        @block.vector
        def _(dve):
            dve.wait_ge(M.small_in, 64)
            dve.wait_ge(std, 1)
            K.dve.link(dve, dve.reciprocal(M.ss[:, 0, :], M.ss[:, 1, :]))
            a, b = ROWC["dckv"]
            for t in range(QT):
                dve.scalar_tensor_tensor(M.rsc[:, 1, t * P:t * P + P], M.rows[:, t, a:b], M.ss[:, 0, t:t + 1],
                                         M.gkv[:, :], ALU.mult, ALU.mult).then_inc(nrm, 1)
            iw = M.rows[:, :, ROWC["iw"][0]:ROWC["iw"][1]]
            dve.tensor_scalar(iw, iw, HEADS ** -0.5 * HD ** -0.5, None, ALU.mult).then_inc(nrm, 1)
            for t in range(QT):
                dve.wait_ge(vdm, t + 1)
                dve.tensor_copy(M.vd[:, t, :], K.ps[3 + t % 2][:, :]).then_inc(cmk, 1)
            for i in range(2):
                dve.wait_ge(hidm, 2 * (i + 1))
                dve.tensor_tensor(M.bias[:, i:i + 1], K.ps[5 + i][:, 64:65], K.p("cmp_b1", i, 1),
                                  ALU.add).then_inc(biasd, 1)
            dve.wait_ge(cmm, 1)
            b2 = K.p("cmp_b2")
            for g in range(2):
                rows = slice(64 * g, 64 * g + 64)
                dve.tensor_scalar(M.kc[rows, :], K.ps[5][rows, 128 + NCMP * g:128 + NCMP * g + NCMP], b2[rows, :],
                                  None, ALU.add)
                dve.wait_ge(cmm, 2)
                dve.tensor_tensor(M.vc[:, g, :], K.ps[6][0:NCMP, 128 + 64 * g:192 + 64 * g], M.b2v[:, :],
                                  ALU.add).then_inc(cmk, 1)

        @block.tensor
        def _(pe):
            pe.wait_ge(nrm, QT)
            for t in range(QT):
                last = pe.transpose(K.ps[0][:, t * P:t * P + P], M.rsc[:, 1, t * P:t * P + P], const(K, "ident"))
            last.then_inc(ct, 1)
            pe.wait_ge(M.small_in, 64)
            pe.wait_ge(ctk, 1)
            for j in range(4):
                if j >= 2:
                    pe.wait_ge(kvk, j - 1)
                pe.matmul(K.ps[1 + j % 2][:, :], M.wuk[:, 2 * j:2 * j + 2, :], M.cT[:, :], start=True, stop=False)
                pe.matmul(K.ps[1 + j % 2][:, :], const(K, "esel", ROPE), M.kr[:, :], start=False,
                          stop=True).then_inc(kdm, 1)
            for t in range(QT):
                if t >= 2:
                    pe.wait_ge(cmk, t - 1)
                pe.matmul(K.ps[3 + t % 2][:, :], M.cT[:, t * P:t * P + P], M.wuv[:, :, :].rearrange("p h d -> p (h d)"),
                          start=True, stop=True).then_inc(vdm, 1)
            pe.wait_ge(kk_in, 16 * 8)
            w = K.ring.take(pe, "cmp").rearrange("p (i m h) -> p i m h", i=2, m=16)
            for i in range(2):
                for m in range(16):
                    rhs = M.kk[:, i, :, 2 * m:2 * m + 16 * (NCMP - 1) + 1:16]
                    last = pe.matmul(K.ps[5 + i][:, 0:2 * NCMP].rearrange("p (g n) -> p g n", g=2), w[:, i, m, :],
                                     rhs, start=(m == 0), stop=(m == 15))
                last.then_inc(hidm, 1)
                for m in range(16):
                    last = pe.matmul(K.ps[5 + i][:, 64:65], w[:, i, m, :], K.p("cmp_pe", 16 * i + m, 1),
                                     start=(m == 0), stop=(m == 15))
                last.then_inc(hidm, 1)
            K.ring.left(hidm, 4)
            pe.wait_ge(hidd, 2)
            pe.wait_ge(w2in, 16 * 3)
            pe.matmul(K.ps[5][:, 128:128 + 2 * NCMP], w2[:, 0:2, :], M.hid[:, 0, :],
                      start=True, stop=True).then_inc(cmm, 1)
            for g in range(2):
                last = pe.matmul(K.ps[6][0:NCMP, 128 + 64 * g:192 + 64 * g], M.hid[:, 1, NCMP * g:NCMP * g + NCMP],
                                 w2[:, 2, :], start=True, stop=True)
            last.then_inc(cmm, 1)

        @block.sync
        def _(sp):
            for i in range(2):
                for g in range(2):
                    src = M.kv[64 * g:64 * g + 64, i, :]
                    sp.dma_start(M.kk[0:64, i, g, :], src).then_inc(kk_in, 16)
                    sp.dma_start(M.kk[64:128, i, g, 0:SEQ - 1], src[:, 1:SEQ]).then_inc(kk_in, 16)
            for n, i in enumerate((0, 0, 1)):
                sp.dma_start(w2[:, n, :], K.A["cmp_w2"][0, i]).then_inc(w2in, 16)
            K.ring.load_ahead(sp)


def indexer(K, M):
    nc = K.nc
    mm, rel, acc, done = (K.sem(f"ix_{n}") for n in ("mm", "relu", "acc", "done"))
    units = [(r, h) for r in range(1, QT) for h in range(HEADS)]
    with nc.Block() as block:

        @block.tensor
        def _(pe):
            for u, (r, h) in enumerate(units):
                rows = slice(64 * (h % 2), 64 * (h % 2) + 64)
                if u >= 4:
                    pe.wait_ge(rel, u - 3)
                pe.matmul(K.ps[u % 4][:, 0:(r + 1) * P], M.iq[rows, h // 2, r * P:r * P + P],
                          M.ik[rows, 0:(r + 1) * P], start=True, stop=True).then_inc(mm, 1)

        @block.scalar
        def _(act):
            for u, (r, h) in enumerate(units):
                act.wait_ge(mm, u + 1)
                if u >= 2:
                    act.wait_ge(acc, u - 1)
                act.activation(M.rsc[:, u % 2, 0:(r + 1) * P], K.ps[u % 4][:, 0:(r + 1) * P], ACT.Relu).then_inc(rel, 1)

        @block.vector
        def _(dve):
            dve.tensor_copy(M.sel[:, 0, 0:P], const(K, "causal")[:, SEQ - P:SEQ]).then_inc(done, 1)
            for u, (r, h) in enumerate(units):
                w = (r + 1) * P
                iw = M.rows[:, r, ROWC["iw"][0] + h:ROWC["iw"][0] + h + 1]
                dve.wait_ge(rel, u + 1)
                if u:
                    dve.wait_ge(acc, u)
                if h == 0:
                    dve.tensor_scalar(M.score[:, 0:w], M.rsc[:, u % 2, 0:w], iw, None, ALU.mult).then_inc(acc, 1)
                else:
                    dve.scalar_tensor_tensor(M.score[:, 0:w], M.rsc[:, u % 2, 0:w], iw, M.score[:, 0:w], ALU.mult,
                                             ALU.add).then_inc(acc, 1)
                if h == HEADS - 1:
                    dve.wait_ge(acc, u + 1)
                    tri = const(K, "causal")[:, SEQ - P:SEQ]
                    K.dve.link(dve, dve.scalar_tensor_tensor(M.score[:, w - P:w], tri, -UNSEEN / -NEG,
                                                             M.score[:, w - P:w], ALU.mult, ALU.add))
                    for _ in range(TOPK // 8):
                        K.dve.link(dve, dve.max(M.top[:, :], M.score[:, 0:w]))
                        K.dve.link(dve, dve.match_replace(M.score[:, 0:w], M.top[:, :], M.score[:, 0:w], TAKEN))
                    K.dve.link(dve, dve.tensor_scalar(M.score[:, 0:w], M.score[:, 0:w], TAKEN, 1.0, ALU.is_equal,
                                                      ALU.subtract))
                    K.dve.link(dve, dve.scalar_tensor_tensor(M.sel[:, r, 0:w], M.score[:, 0:w], -NEG,
                                                             const(K, "causal")[:, SEQ - w:SEQ], ALU.mult, ALU.add))

def compressed_probs(K, M):
    nc = K.nc
    mm, cen, ex, pr, tr, kept = (K.sem(f"cp_{n}") for n in ("mm", "centred", "exp", "probs", "turn", "kept"))

    with nc.Block() as block:

        @block.tensor
        def _(pe):
            def scores(r):
                if r >= 2:
                    pe.wait_ge(cen, r - 1)
                for g in range(2):
                    rows = slice(64 * g, 64 * g + 64)
                    for j in range(4):
                        last = pe.matmul(K.ps[2 * (r % 2) + g][:, NCMP * j:NCMP * j + NCMP],
                                         M.q[rows, j, r * P:r * P + P], M.kc[rows, :], start=True, stop=True)
                    last.then_inc(mm, 1)

            scores(0)
            for r in range(QT):
                if r + 1 < QT:
                    scores(r + 1)
                pe.wait_ge(pr, r + 1)
                for half in range(2):
                    i = 2 * r + half
                    if i >= 3:
                        pe.wait_ge(kept, i - 2)
                    for h in range(4):
                        last = pe.transpose(K.ps[4 + i % 3][0:NCMP, h * P:h * P + P], M.pc[:, r % 2, 4 * half + h, :],
                                            const(K, "ident"))
                    last.then_inc(tr, 1)

        @block.scalar
        def _(act):
            def turned(r):
                for half in range(2):
                    i = 2 * r + half
                    act.wait_ge(tr, i + 1)
                    act.activation(M.pct[:, r, 4 * half:4 * half + 4, :],
                                   K.ps[4 + i % 3][0:NCMP, :].rearrange("p (h q) -> p h q", h=4),
                                   ACT.Copy).then_inc(kept, 1)
            for r in range(QT):
                act.wait_ge(cen, r + 1)
                act.activation(M.pc[:, r % 2], M.pc[:, r % 2], ACT.Exp, scale=SCALE).then_inc(ex, 1)
                if r >= 1:
                    turned(r - 1)
            turned(QT - 1)

        @block.vector
        def _(dve):
            for r in range(QT):
                pc, mx = M.pc[:, r % 2], M.pcs[:, 0, :]
                add = const(K, "cmp_add")[:, r * NCMP:r * NCMP + NCMP].unsqueeze(1).broadcast_to([P, HEADS, NCMP])
                one = const(K, "cmp_one")[:, r * NCMP:r * NCMP + NCMP].unsqueeze(1).broadcast_to([P, HEADS, NCMP])
                sm = M.pcs[:, 1, :]
                dve.wait_ge(mm, 2 * r + 2)
                if r >= 2:
                    dve.wait_ge(tr, 2 * (r - 1))
                for g in range(2):
                    s = slice(4 * g, 4 * g + 4)
                    K.dve.link(dve, dve.tensor_tensor(
                        pc[:, s], K.ps[2 * (r % 2) + g][:, 0:4 * NCMP].rearrange("p (h n) -> p h n", h=4), add[:, s],
                        ALU.add))
                K.dve.link(dve, dve.tensor_reduce(mx, pc, AX.X, ALU.max))
                dve.tensor_tensor(pc, pc, mx.unsqueeze(2).broadcast_to([P, HEADS, NCMP]), ALU.subtract).then_inc(cen, 1)
                dve.wait_ge(ex, r + 1)
                K.dve.link(dve, dve.tensor_tensor(pc, pc, one, ALU.mult))
                K.dve.link(dve, dve.tensor_reduce(sm, pc, AX.X, ALU.add))
                K.dve.link(dve, dve.tensor_scalar(sm, sm, 1e-30, None, ALU.max))
                K.dve.link(dve, dve.reciprocal(mx, sm))
                gate = M.rows[:, r, ROWC["gate"][0]:ROWC["gate"][0] + HEADS]
                K.dve.link(dve, dve.tensor_tensor(mx, mx, gate, ALU.mult))
                dve.tensor_tensor(pc, pc, mx.unsqueeze(2).broadcast_to([P, HEADS, NCMP]), ALU.mult).then_inc(pr, 1)
                dve.wait_ge(pr, r + 1)


def attention(K, M):
    nc = K.nc
    qk, mxd, ex, pd, tr, ptk, pv, ok = (K.sem(f"at_{n}") for n in (
        "qk", "max", "exp", "probs", "turn", "turned", "pv", "out"))
    units = []
    for r in range(QT):
        for j in range(8):
            for half in range(2):
                units += [(r, j, half, b) for b in (("slc", "win") if j < 4 else ("dsa",))]
    outs = {}
    for u, (r, j, half, b) in enumerate(units):
        outs[(r, j)] = u + 1
    order = list(outs)

    def operands(u):
        r, j, half, b = units[u]
        rows = slice(64 * half, 64 * half + 64)
        if b == "dsa":
            head = 2 * (j - 4) + half
            return (M.dq[rows, j - 4, r * P:r * P + P], M.kd[rows, j - 4, :],
                    lambda c: M.vd[:, c, 64 * head:64 * head + 64])
        col = ROWC["nvs" if b == "slc" else "nvw"][0] + 64 * half
        return (M.q[rows, j, r * P:r * P + P], M.kv[rows, 2 if b == "slc" else 3, :],
                lambda c: M.rows[:, c, col:col + 64])

    with nc.Block() as block:

        @block.tensor
        def _(pe):
            def scores(u):
                r = units[u][0]
                q, k, _ = operands(u)
                if u >= 2:
                    pe.wait_ge(mxd, u - 1)
                pe.matmul(K.ps[u % 2][:, 0:(r + 1) * P], q, k[:, 0:(r + 1) * P], start=True,
                          stop=True).then_inc(qk, 1)

            def turn(u):
                r = units[u][0]
                pe.wait_ge(pd, u + 1)
                if u >= 2:
                    pe.wait_ge(ptk, u - 1)
                for c in range(r + 1):
                    last = pe.transpose(K.ps[2 + u % 2][:, c * P:c * P + P], M.p[u % 3][:, c * P:c * P + P],
                                        const(K, "ident"))
                last.then_inc(tr, 1)

            def values(u):
                r, j, half, b = units[u]
                n = order.index((r, j))
                bank = K.ps[4 + n % 2][64 * half:64 * half + 64, 0:P]
                if n >= 2 and half == 0 and b != "win":
                    pe.wait_ge(ok, n - 1)
                if b == "slc":
                    pe.matmul(bank, M.vc[:, half, :], M.pct[:, r, 4 * half + j, :], start=True, stop=False)
                pe.wait_ge(ptk, u + 1)
                v = operands(u)[2]
                for c in range(r + 1):
                    last = pe.matmul(bank, v(c), M.pt[:, u % 2, c * P:c * P + P], start=(b == "dsa" and c == 0),
                                     stop=(b != "slc" and c == r))
                last.then_inc(pv, 1)

            for u in range(len(units) + 3):
                if u < len(units):
                    scores(u)
                if 2 <= u < len(units) + 2:
                    turn(u - 2)
                if u >= 3:
                    values(u - 3)

        @block.vector
        def _(dve):
            def maximum(u):
                r, j, half, b = units[u]
                w = (r + 1) * P
                mask = M.sel[:, r, 0:w] if b == "dsa" else const(K, "causal")[:, SEQ - w:SEQ]
                dve.wait_ge(qk, u + 1)
                if u >= 3:
                    dve.wait_ge(tr, u - 2)
                dve.tensor_tensor_reduce(M.p[u % 3][:, 0:w], K.ps[u % 2][:, 0:w], mask, -SCALE, 3.0e38, ALU.add,
                                         ALU.min, M.stat[:, u % 3, 0:1]).then_inc(mxd, 1)

            def normalise(u):
                r, j, half, b = units[u]
                w = (r + 1) * P
                st = M.stat[:, u % 3, :]
                dve.wait_ge(ex, u + 1)
                K.dve.link(dve, dve.reciprocal(st[:, 2:3], st[:, 1:2]))
                if b == "dsa":
                    dve.tensor_scalar(M.p[u % 3][:, 0:w], M.p[u % 3][:, 0:w], st[:, 2:3], None,
                                      ALU.mult).then_inc(pd, 1)
                else:
                    g = ROWC["gate"][0] + HEADS * (1 if b == "slc" else 2) + 4 * half + j
                    dve.tensor_scalar(M.p[u % 3][:, 0:w], M.p[u % 3][:, 0:w], st[:, 2:3], M.rows[:, r, g:g + 1],
                                      ALU.mult, ALU.mult).then_inc(pd, 1)

            for u in range(len(units) + 1):
                if u < len(units):
                    maximum(u)
                if u >= 1:
                    normalise(u - 1)

        @block.scalar
        def _(act):
            def turned(u):
                r = units[u][0]
                act.wait_ge(tr, u + 1)
                if u >= 2:
                    act.wait_ge(pv, u - 1)
                act.activation(M.pt[:, u % 2, 0:(r + 1) * P], K.ps[2 + u % 2][:, 0:(r + 1) * P],
                               ACT.Copy).then_inc(ptk, 1)

            def output(u):
                r, j, half, b = units[u]
                n = order.index((r, j))
                if outs[(r, j)] == u + 1:
                    act.wait_ge(pv, u + 1)
                    act.activation(K.h[:, j, CTX + r * P:CTX + r * P + P], K.ps[4 + n % 2][:, 0:P],
                                   ACT.Copy).then_inc(ok, 1)

            for u in range(len(units) + 4):
                if u < len(units):
                    r = units[u][0]
                    act.wait_ge(mxd, u + 1)
                    p = M.p[u % 3][:, 0:(r + 1) * P]
                    act.activation(p, p, ACT.Exp, bias=M.stat[:, u % 3, 0:1], scale=-1.0,
                                   accum_out=M.stat[:, u % 3, 1:2]).then_inc(ex, 1)
                if 2 <= u < len(units) + 2:
                    turned(u - 2)
                if 4 <= u:
                    output(u - 4)

        @block.sync
        def _(sp):
            K.ring.load_ahead(sp)


def coefs_1(K):
    nc = K.nc
    done = K.sem("coef1_done")
    with nc.Block() as block:

        @block.vector
        def _(dve):
            dve.wait_ge(K.mod_mm, 12)
            dve.tensor_tensor(K.mod1[:, 16:48], K.ps[7][:, 16:48], K.p("b_ada", 16, 32), ALU.add).then_inc(done, 1)
            dve.wait_ge(done, 1)
            dve.tensor_tensor(K.coef[:, 1], K.mod1[:, 16:24], K.p("g_post_mix"), ALU.mult).then_inc(done, 1)
            dve.scalar_tensor_tensor(K.coef[:, 2], K.mod1[:, 32:40], 1.0, K.p("g_pre_ffn"), ALU.add,
                                     ALU.mult).then_inc(done, 1)
            dve.tensor_tensor(K.coef[:, 3], K.mod1[:, 40:48], K.p("g_post_ffn"), ALU.mult).then_inc(done, 1)


def coefs_2(K):
    nc = K.nc
    done = K.sem("coef2_done")
    with nc.Block() as block:

        @block.vector
        def _(dve):
            b = K.p("b_mod_2").unsqueeze(2).broadcast_to([P, 72, 2])
            dve.wait_ge(K.mod_mm, 30)
            dve.tensor_tensor(K.mod2[:, :, :], K.ps[7][:, 48:192].rearrange("p (j v) -> p j v", v=2), b,
                              ALU.add).then_inc(done, 1)
            dve.wait_ge(done, 1)
            for j in range(3):
                m = K.mod2[:, 8 * (3 * j + 1):8 * (3 * j + 1) + 8, :]
                dve.scalar_tensor_tensor(K.coef[:, 4 + j], m[:, :, 0], 1.0, K.p("norm_pre_2", 8 * j, 8), ALU.add,
                                         ALU.mult).then_inc(done, 1)
                if j < 2:
                    dve.scalar_tensor_tensor(K.coef[:, 7 + j], m[:, :, 1], 1.0, K.p("norm_pre_2", 8 * j, 8),
                                             ALU.add, ALU.mult).then_inc(done, 1)
                w = K.mod2[:, 8 * (3 * j + 2):8 * (3 * j + 2) + 8, :]
                dve.scalar_tensor_tensor(K.coef[:, 9 + j], w[:, :, 0], 1.0 if j == 1 else 0.5,
                                         K.p("norm_post_2", 8 * j, 8), ALU.mult, ALU.mult).then_inc(done, 1)
            dve.scalar_tensor_tensor(K.cc1[:, :], K.mod2[:, 16:24, 1], 0.5, K.p("norm_post_2", 0, 8), ALU.mult,
                                     ALU.mult).then_inc(done, 1)


def project_out(K, name, y, call):
    nc = K.nc
    mm, kept = K.sem(f"po_mm{call}"), K.sem(f"po_kept{call}")
    with nc.Block() as block:

        @block.tensor
        def _(pe):
            for d in range(KT):
                if d % 4 == 0:
                    w = K.ring.take(pe, (name, d // 4)).rearrange("p (k n) -> p k n", k=KT)
                if d >= 3:
                    pe.wait_ge(kept, d - 2)
                for k in range(KT):
                    last = pe.matmul(K.ps[d % 3][:, :], w[:, k, (d % 4) * P:(d % 4) * P + P], K.h[:, k, CTX:TOK],
                                     start=(k == 0), stop=(k == KT - 1))
                last.then_inc(mm, 1)
                if d % 4 == 3:
                    K.ring.left(mm, d + 1)

        @block.scalar
        def _(act):
            for d in range(KT):
                act.wait_ge(mm, d + 1)
                act.activation(y[:, d, :], K.ps[d % 3][:, :], ACT.Copy).then_inc(kept, 1)

        @block.sync
        def _(sp):
            K.ring.load_ahead(sp)


def ffn(K, call, with_ctx):
    nc, S = K.nc, K.ffn_sems
    parts = [(CTX, SEQ)] + ([(0, CTX)] if with_ctx else [])
    mods = {(0, 0): (11, 12), (0, 1): (13,), (0, 2): (14,), (1, 0): (15,), (1, 1): (16,), (1, 2): (17,)} \
        if call == 0 else {}
    with ExitStack() as st:
        hid = K.sb(f"hidden{call}", [P, FT, TOK if with_ctx else SEQ], st)
        off = 0 if with_ctx else CTX
        sg = K.sb(f"silu{call}", [P, 2, TOK], st)

        def up_bank(f, which, part):
            if part == 0:
                return K.ps[2 * (f % 2) + which][:, :]
            return K.ps[4 + 2 * (f % 2) + which][:, 0:CTX]

        with nc.Block() as block:

            @block.tensor
            def _(pe):
                for g in range(FT // 2):
                    w = K.ring.take(pe, ("up", call, g)).rearrange("p (k h n) -> p k h n", k=KT, h=2)
                    for i in range(2):
                        f = 2 * g + i
                        if f >= 2:
                            S["hid"].wait(pe, f - 1)
                        for which in range(2):
                            for k in range(KT):
                                for n, (a, m) in enumerate(parts):
                                    last = pe.matmul(up_bank(f, which, n), w[:, k, which, i * P:i * P + P],
                                                     K.h[:, k, a:a + m], start=(k == 0), stop=(k == KT - 1))
                            last.then_inc(S["up_mm"].sem, 1)
                    K.ring.left(S["up_mm"].sem, S["up_mm"].base + 4 * g + 4)
                    if mods and g:
                        modulation_columns(K, pe, ("mod", g - 1))
                for half in range(2):
                    for s in range(3):
                        w = K.ring.take(pe, ("down", call, half, s)).rearrange("p (f n) -> p f n", n=512)
                        for f in range(8 * s, min(8 * s + 8, FT)):
                            if half == 0:
                                S["hid"].wait(pe, max(f + 1, FT if f == 0 else 0))
                            for d in range(4):
                                if half == 1 and f == 0:
                                    S["down_out"].wait(pe, d + 1)
                                for n, (a, m) in enumerate(parts):
                                    last = pe.matmul(K.ps[4 * n + d][:, 0:m], w[:, f - 8 * s, d * P:d * P + P],
                                                     hid[:, f, a - off:a - off + m], start=(f == 0),
                                                     stop=(f == FT - 1))
                                if f == FT - 1:
                                    last.then_inc(S["down_mm"].sem, 1)
                        if s == 2:
                            K.ring.left(S["down_mm"].sem, S["down_mm"].base + 4 * half + 4)
                        else:
                            K.ring.free(last)
                        for m in mods[(half, s)] if mods else ():
                            modulation_columns(K, pe, ("mod", m - 1))
                if mods:
                    modulation_columns(K, pe, ("mod", 17))

            @block.scalar
            def _(act):
                for f in range(FT):
                    S["up_mm"].wait(act, 2 * f + 1)
                    if f >= 2:
                        S["hid"].wait(act, f - 1)
                    for n, (a, m) in enumerate(parts):
                        last = act.activation(sg[:, f % 2, a:a + m], up_bank(f, 0, n), ACT.Silu)
                    last.then_inc(S["silu"].sem, 1)

            @block.vector
            def _(dve):
                for f in range(FT):
                    S["up_mm"].wait(dve, 2 * f + 2)
                    S["silu"].wait(dve, f + 1)
                    for n, (a, m) in enumerate(parts):
                        last = dve.tensor_tensor(hid[:, f, a - off:a - off + m], up_bank(f, 1, n),
                                                 sg[:, f % 2, a:a + m], ALU.mult)
                    last.then_inc(S["hid"].sem, 1)
                    if mods and f % 2:
                        modulation_sums(K, dve, ("mod", f // 2))
                for half in range(2):
                    for s in range(3) if mods else ():
                        for m in mods[(half, s)]:
                            modulation_sums(K, dve, ("mod", m))
                    for d in range(4):
                        S["down_mm"].wait(dve, 4 * half + d + 1)
                        for n, (a, m) in enumerate(parts):
                            last = dve.tensor_copy(K.h[:, 4 * half + d, a:a + m], K.ps[4 * n + d][:, 0:m])
                        last.then_inc(S["down_out"].sem, 1)

            @block.sync
            def _(sp):
                K.ring.load_ahead(sp)

        S["up_mm"].close(2 * FT)
        S["silu"].close(FT)
        S["hid"].close(FT)
        S["down_mm"].close(KT)
        S["down_out"].close(KT)


def stage_ffn_1(K, out):
    ffn(K, 0, False)
    coefs_2(K)
    rms_norms(K, [norm_out(lat(K.h), SEQ, K.coef[:, 3], lat(K.x)),
                  norm_in(ctxt(K.x), CTX, K.coef[:, 7], K.mod2[:, 0:8, 1], ctxt(K.h)),
                  norm_in(lat(K.x), SEQ, K.coef[:, 4], K.mod2[:, 0:8, 0], lat(K.h), after=True)])


def stage_ffn_2(K, out):
    ffn(K, 1, True)
    rms_norms(K, [norm_out(lat(K.h), SEQ, K.coef[:, 9], lat(K.x)),
                  norm_out(ctxt(K.h), CTX, K.cc1, ctxt(K.x)),
                  norm_in(lat(K.x), SEQ, K.coef[:, 5], K.mod2[:, 24:32, 0], lat(K.h), after=True),
                  norm_in(ctxt(K.x), CTX, K.coef[:, 8], K.mod2[:, 24:32, 1], ctxt(K.h), after=True)])


DIRS = {0: list(range(CH)), 1: [c for c in range(CC)][::-1] + [c for c in range(CC, CH)][::-1]}


def stage_mixer_2(K, out):
    with ExitStack() as st:
        M = Fields()
        M.q = K.sb("mq_t", [P, MH, SEQ], st)
        M.k = K.sb("mk_t", [P, MH, SEQ], st)
        M.kr = K.sb("mk_rows", [P, CH, MH, P], st)
        M.v = K.sb("mv_rows", [P, CH, MH, P + 1], st)
        M.o = K.sb("mo_t", [P, MH, SEQ], st)
        M.rw = K.sb("m_rcol", [P, 2, CH, 2, MH], st)
        M.old = K.sb("m_old", [MH, 2 * CH], st)
        M.oldc = K.sb("m_oldc", [P, MH, 2 * CH], st)
        M.gr = K.sb("gate_rows", [P, CH, 16], st)
        with ExitStack() as st2:
            M.u = K.sb("mu_t", [P, MH, TOK], st2)
            M.pool = K.sb("pool_t", [P, 4, SEQ], st2)
            M.gw = K.sb("gate_w", [P, KT, 16], st2)
            M.ic = K.h[:, 0:4, CTX:TOK]
            M.wq = [K.h[:, MH:2 * MH, P * i:P * i + P] for i in range(2)]
            M.pw = K.h[:, 0:4, 0:P]
            project_2(K, M)
            conv_pool(K, M)
        M.bc = K.sb("m_bc", [MH, 2, CH, 3, P], st)
        gates(K, M)
        mlstm(K, M)
    with ExitStack() as st:
        y = K.sb("mix_out2", [P, KT, SEQ], st)
        project_out(K, "out2", y, 1)
        rms_norms(K, [norm_out(lambda k: y[:, k, :], SEQ, K.coef[:, 10], lat(K.x)),
                      norm_in(lat(K.x), SEQ, K.coef[:, 6], K.mod2[:, 48:56, 0], lat(K.h), after=True)])


def project_2(K, M):
    nc, A = K.nc, K.A
    mm, kept, rmm, rk = (K.sem(f"p2_{n}") for n in ("mm", "kept", "rmm", "rkept"))
    M.w_in = K.sem("m2_w_in")
    tiles = [("u", j) for j in range(4)] + [("o", j) for j in range(4)] + [("pool", j) for j in range(4)]
    with nc.Block() as block:

        @block.tensor
        def _(pe):
            i = 0
            for item in ("u", "v", "o", "pool"):
                w = K.ring.take(pe, item).rearrange("p (k n) -> p k n", k=KT)
                if item == "v":
                    pe.wait_ge(M.w_in, 16)
                    for c in range(CH):
                        if c >= 2:
                            pe.wait_ge(rk, c - 1)
                        for k in range(KT):
                            x = K.h[:, k, c * P:c * P + P]
                            pe.matmul(K.ps[4 + c % 2][:, :], x, w[:, k, :], start=(k == 0), stop=(k == KT - 1))
                            last = pe.matmul(K.ps[6 + c % 2][:, 0:16], x, M.gw[:, k, :], start=(k == 0),
                                             stop=(k == KT - 1))
                        last.then_inc(rmm, 1)
                else:
                    for j in range(4):
                        if i >= 2:
                            pe.wait_ge(kept, i - 1)
                        for k in range(KT):
                            wt = w[:, k, j * P:j * P + P]
                            last = pe.matmul(K.ps[i % 2][:, :], wt, K.h[:, k, CTX:TOK], start=(k == 0),
                                             stop=(k == KT - 1))
                            if item == "u":
                                last = pe.matmul(K.ps[2 + i % 2][:, 0:CTX], wt, K.h[:, k, 0:CTX], start=(k == 0),
                                                 stop=(k == KT - 1))
                        last.then_inc(mm, 1)
                        i += 1
                if item == "v":
                    K.ring.left(rmm, CH)
                else:
                    K.ring.left(mm, i)

        @block.scalar
        def _(act):
            for i, (item, j) in enumerate(tiles):
                act.wait_ge(mm, i + 1)
                if item == "u":
                    act.activation(M.u[:, j, 0:CTX], K.ps[2 + i % 2][:, 0:CTX], ACT.Copy)
                    act.activation(M.u[:, j, CTX:TOK], K.ps[i % 2][:, :], ACT.Copy).then_inc(kept, 1)
                elif item == "o":
                    act.activation(M.o[:, j, :], K.ps[i % 2][:, :], ACT.Sigmoid).then_inc(kept, 1)
                else:
                    act.activation(M.pool[:, j, :], K.ps[i % 2][:, :], ACT.Copy).then_inc(kept, 1)

        @block.vector
        def _(dve):
            dve.memset(M.v[:, :, :, P:P + 1], 1.0)
            for c in range(CH):
                dve.wait_ge(rmm, c + 1)
                dve.tensor_copy(M.v[:, c, :, 0:P], K.ps[4 + c % 2][:, :].rearrange("p (h v) -> p h v", h=MH))
                dve.tensor_copy(M.gr[:, c, :], K.ps[6 + c % 2][:, 0:16]).then_inc(rk, 1)

        @block.sync
        def _(sp):
            sp.dma_start(M.gw[:, :, :], A["w_in_2"][0].rearrange("(k p) n -> p k n", p=P)[:, :, M_G:M_POOL]).then_inc(M.w_in, 16)
            K.ring.load_ahead(sp)


def conv_pool(K, M):
    nc = K.nc
    cv, sl, qm, qk, km, kk, pl, pm, pk, ic_in = (K.sem(f"cv_{n}") for n in (
        "conv", "silu", "qmm", "qkept", "kmm", "kkept", "pool", "pmm", "pkept", "counts"))
    ROWS_G, COLS_G, PAD = SEQ // 64, 64, 16
    with ExitStack() as st, nc.Block() as block:
        cu = [t[:, :, :].rearrange("p a b -> p (a b)")[:, 0:TOK] for t in (K.sq, K.tmp)]
        us = M.u
        pc = K.sb("pool_cols", [P, ROWS_G, COLS_G + PAD], st)
        pr = K.sb("pool_rows", [P, ROWS_G + PAD, COLS_G], st)
        pa = K.sb("pool_a", [P, (ROWS_G + PAD) * COLS_G], st)
        pac = pa[:, 0:ROWS_G * (COLS_G + PAD)].rearrange("p (r c) -> p r c", r=ROWS_G)
        par = pa[:, :].rearrange("p (r c) -> p r c", c=COLS_G)
        pd = K.h[:, MH:2 * MH, CTX:TOK]

        @block.sync
        def _(sp):
            sp.dma_start(M.wq[0], K.A["w_q_2"][0].rearrange("h d e -> d h e")).then_inc(M.w_in, 16)
            sp.dma_start(M.wq[1], K.A["w_k_2"][0].rearrange("h d e -> d h e")).then_inc(M.w_in, 16)
            sp.dma_start(M.pw, K.A["pool_w_2"][0].rearrange("g c d -> c g d")).then_inc(M.w_in, 16)
            sp.dma_start(M.ic, K.A["inv_count"].rearrange("o (g n) -> o g n", g=4).broadcast_to([P, 4, SEQ])).then_inc(
                ic_in, 16)

        @block.vector
        def _(dve):
            for h in range(MH):
                w = lambda j: K.p("conv_w_2", 4 * j + h, 1)
                o = cu[h % 2]
                u = M.u[:, h, :]
                if h >= 2:
                    dve.wait_ge(sl, h - 1)
                K.dve.link(dve, dve.tensor_scalar(o, u, w(1), K.p("conv_b_2", h, 1), ALU.mult, ALU.add))
                for a, b in ((0, CTX), (CTX, TOK)):
                    K.dve.link(dve, dve.scalar_tensor_tensor(o[:, a + 1:b], u[:, a:b - 1], w(0), o[:, a + 1:b],
                                                             ALU.mult, ALU.add))
                    last = dve.scalar_tensor_tensor(o[:, a:b - 1], u[:, a + 1:b], w(2), o[:, a:b - 1], ALU.mult,
                                                    ALU.add)
                    if a == 0:
                        K.dve.link(dve, last)
                last.then_inc(cv, 1)
            step = lambda ins: K.dve.link(dve, ins)
            dve.wait_ge(ic_in, 16)
            for g in range(4):
                win = 2 ** (g + 1)
                lo = win // 2
                step(dve.memset(pc[:, :, :], 0.0))
                step(dve.tensor_copy(pc[:, :, lo:lo + COLS_G], M.pool[:, g, :].rearrange("p (r c) -> p r c", c=COLS_G)))
                n = COLS_G + PAD
                src = pc
                s = 1
                bufs = [pac, pc[:, :, :]]
                cur = bufs[1]
                while s < win:
                    n -= s
                    dst = bufs[0] if cur is not bufs[0] else bufs[1]
                    step(dve.tensor_tensor(dst[:, :, 0:n], cur[:, :, 0:n], cur[:, :, s:s + n], ALU.add))
                    cur, s = dst, 2 * s
                step(dve.memset(pr[:, :, :], 0.0))
                step(dve.tensor_copy(pr[:, lo:lo + ROWS_G, :], cur[:, :, 0:COLS_G]))
                n, s = ROWS_G + PAD, 1
                bufs = [par, pr[:, :, :]]
                cur = bufs[1]
                while s < win:
                    n -= s
                    dst = bufs[0] if cur is not bufs[0] else bufs[1]
                    step(dve.tensor_tensor(dst[:, 0:n, :], cur[:, 0:n, :], cur[:, s:s + n, :], ALU.add))
                    cur, s = dst, 2 * s
                d = pd[:, g, :].rearrange("p (r c) -> p r c", c=COLS_G)
                step(dve.tensor_tensor(d, cur[:, 0:ROWS_G, :], M.ic[:, g, :].rearrange("p (r c) -> p r c", c=COLS_G),
                                        ALU.mult))
                dve.tensor_tensor(pd[:, g, :], pd[:, g, :], M.pool[:, g, :], ALU.subtract).then_inc(pl, 1)

        @block.scalar
        def _(act):
            for h in range(MH):
                act.wait_ge(cv, h + 1)
                act.activation(us[:, h, :], cu[h % 2], ACT.Silu).then_inc(sl, 1)
            for i in range(2 * MH):
                act.wait_ge(qm, i + 1)
                h = i // 2
                act.activation((M.q if i % 2 == 0 else M.k)[:, h, :], K.ps[i % 2][:, :], ACT.Copy,
                               scale=1.0 if i % 2 == 0 else P ** -0.5).then_inc(qk, 1)
            for c in range(CH):
                act.wait_ge(km, c + 1)
                act.activation(M.kr[:, c].rearrange("p h d -> p (h d)"), K.ps[2 + c % 2][:, :], ACT.Copy,
                               scale=P ** -0.5).then_inc(kk, 1)
            for g in range(4):
                act.wait_ge(pm, g + 1)
                act.activation(K.h[:, MH + g, CTX:TOK], K.ps[4 + g % 2][:, :], ACT.Copy,
                               scale=K.p("pool_scale_2", g, 1)).then_inc(pk, 1)

        @block.tensor
        def _(pe):
            pe.wait_ge(M.w_in, 16 * 4)
            for i in range(2 * MH):
                h = i // 2
                pe.wait_ge(sl, h + 1)
                if i >= 2:
                    pe.wait_ge(qk, i - 1)
                pe.matmul(K.ps[i % 2][:, :], M.wq[i % 2][:, h, :], us[:, h, CTX:TOK], start=True,
                          stop=True).then_inc(qm, 1)
            for c in range(CH):
                if c >= 2:
                    pe.wait_ge(kk, c - 1)
                for h in range(MH):
                    last = pe.matmul(K.ps[2 + c % 2][:, h * P:h * P + P], us[:, h, c * P:c * P + P], M.wq[1][:, h, :],
                                     start=True, stop=True)
                last.then_inc(km, 1)
            for g in range(4):
                pe.wait_ge(pl, g + 1)
                if g >= 2:
                    pe.wait_ge(pk, g - 1)
                pe.matmul(K.ps[4 + g % 2][:, :], M.pw[:, g, :], pd[:, g, :], start=True, stop=True).then_inc(pm, 1)


def gates(K, M):
    nc, A = K.nc, K.A
    bias_in, tr, g0, a1, st_, tb, done = (K.sem(f"gt_{n}") for n in ("bias", "turn", "dve", "act", "chunk", "back", "done"))
    with ExitStack() as st, nc.Block() as block:
        bias = K.sb("g_bias", [MH, 2, 2], st)
        g = K.sb("g_t", [MH, 4, TOK], st)
        ln = K.sb("g_ln", [MH, 2, TOK], st)
        one = K.sb("g_one", [MH, P], st)
        b = ln
        cm = g[:, 2:4, :]
        mi = K.sb("g_m", [MH, 2, CH + 1], st)
        wk = ln

        @block.sync
        def _(sp):
            for i, src in enumerate((A["i_bias_2"], A["f_bias_2"])):
                sp.dma_start(bias[:, i, :], src[0].rearrange("d h -> h d"),
                             allow_slow_non_contiguous=True).then_inc(bias_in, 16)

        @block.tensor
        def _(pe):
            for c in range(CH):
                if c >= 4:
                    pe.wait_ge(g0, c - 3)
                for kind in range(4):
                    last = pe.transpose(K.ps[c % 4][0:MH, kind * P:kind * P + P], M.gr[:, c, 4 * kind:4 * kind + 4],
                                        const(K, "ident"))
                last.then_inc(tr, 1)
            pe.wait_ge(a1, 3)
            for d in range(2):
                for c in range(CH):
                    s = slice(c * P, c * P + P)
                    pe.transpose(K.ps[4][:, (d * CH + c) * 8:(d * CH + c) * 8 + 4], g[:, d, s],
                                 const(K, "ident")[0:MH, 0:MH])
                    pe.transpose(K.ps[4][:, (d * CH + c) * 8 + 4:(d * CH + c) * 8 + 8], wk[:, d, s],
                                 const(K, "ident")[0:MH, 0:MH])
            for j in range(MH):
                last = pe.matmul(K.ps[5][:, 2 * CH * j:2 * CH * j + 2 * CH],
                                 const(K, "ident")[0:MH, j:j + 1].broadcast_to([MH, P]), M.old[:, :], start=True,
                                 stop=True)
            last.then_inc(tb, 1)

        @block.vector
        def _(dve):
            link = lambda ins: K.dve.link(dve, ins)
            link(dve.memset(one[:, :], 1.0))
            link(dve.memset(mi[:, :, :], 0.0))
            for c in range(CH):
                dve.wait_ge(tr, c + 1)
                dve.tensor_copy(g[:, :, c * P:c * P + P],
                                K.ps[c % 4][0:MH, :].rearrange("h (k t) -> h k t", k=4)).then_inc(g0, 1)
            dve.wait_ge(g0, CH)
            dve.wait_ge(bias_in, 32)
            for d in range(2):
                link(dve.tensor_scalar(g[:, d, :], g[:, d, :], bias[:, 0, d:d + 1], None, ALU.add))
                link(dve.tensor_scalar(g[:, 2 + d, :], g[:, 2 + d, :], bias[:, 1, d:d + 1], None, ALU.add))
            dve.sem_inc(g0, 1)
            dve.wait_ge(a1, 1)
            link(dve.scalar_tensor_tensor(g[:, 2:4, :], g[:, 2:4, :], 0.0, ln[:, :, :], ALU.min, ALU.subtract))
            for d in range(2):
                for c in range(CH):
                    s = slice(c * P, c * P + P) if d == 0 else slice(c * P + P - 1, c * P - 1 if c else None, -1)
                    link(dve.tensor_tensor_scan(b[:, d, s], one[:, :], g[:, 2 + d, s], 0.0, ALU.mult, ALU.add))
            link(dve.tensor_tensor(g[:, 0:2, :], g[:, 0:2, :], b[:, :, :], ALU.subtract))
            for n in range(CH):
                for d in range(2):
                    c = DIRS[d][n]
                    end = c * P + (P - 1 if d == 0 else 0)
                    s = slice(c * P, c * P + P) if d == 0 else slice(c * P + P - 1, c * P - 1 if c else None, -1)
                    f = slice(c * P, c * P + P)
                    m = mi[:, d, n:n + 1]
                    link(dve.tensor_tensor_scan(cm[:, d, s], g[:, d, s], g[:, d, s], m, ALU.max, ALU.max))
                    link(dve.tensor_tensor(mi[:, d, n + 1:n + 2], b[:, d, end:end + 1], cm[:, d, end:end + 1], ALU.add))
                    link(dve.tensor_scalar(M.bc[:, d, c, 0, :], cm[:, d, f], -1.0, None, ALU.mult))
                    link(dve.tensor_scalar(M.bc[:, d, c, 1, :], M.bc[:, d, c, 0, :], m, None, ALU.add))
                    link(dve.tensor_tensor(M.bc[:, d, c, 2, :], M.bc[:, d, c, 0, :], b[:, d, f], ALU.subtract))
            dve.sem_inc(st_, 1)
            dve.wait_ge(tb, 1)
            dve.tensor_copy(M.rw[:, :, :, :, :].rearrange("p d c w h -> p (d c w h)"), K.ps[4][:, 0:2 * CH * 8])
            dve.tensor_copy(M.oldc[:, :, :].rearrange("p h c -> p (h c)"), K.ps[5][:, 0:MH * 2 * CH])

        @block.scalar
        def _(act):
            act.wait_ge(g0, CH + 1)
            K.act.link(act, act.activation(ln[:, :, :], g[:, 2:4, :], ACT.Abs))
            K.act.link(act, act.activation(ln[:, :, :], ln[:, :, :], ACT.Exp, scale=-1.0))
            act.activation(ln[:, :, :], ln[:, :, :], ACT.Ln, bias=1.0).then_inc(a1, 1)
            act.wait_ge(st_, 1)
            for d in range(2):
                for c in range(CH):
                    e = P - 1 if d == 0 else 0
                    act.activation(wk[:, d, c * P:c * P + P], g[:, d, c * P:c * P + P], ACT.Exp,
                                   bias=M.bc[:, d, c, 0, e:e + 1])
                last = act.activation(M.old[:, d * CH:d * CH + CH],
                                      M.bc[:, d, :, 1, P - 1 if d == 0 else 0], ACT.Exp)
                last.then_inc(a1, 1)


def mlstm(K, M):
    nc = K.nc
    sem = {n: K.sem(f"ml_{n}") for n in ("qk", "qkk", "bc", "bc2", "w", "ew", "s", "nd", "den", "h", "wk", "u", "st",
                                         "sq", "ss", "sd", "hn", "c0")}
    with ExitStack() as st:
        qk = K.sb("m_qk", [P, QT, MH, P], st)
        w = K.sb("m_w", [P, MH, P], st)
        s_ = K.sb("m_s", [P, MH, P], st)
        qs = K.sb("m_qs", [P, MH, P], st)
        dn = K.sb("m_dn", [P, MH, P], st)
        wk = K.sb("m_wk", [P, MH, P], st)
        C = K.sb("m_state", [P, MH, P + 1], st)
        H = K.h[:, 0:MH, CTX:TOK]
        steps = []
        for d in range(2):
            steps += [(d, c, n) for n, c in enumerate(DIRS[d])]
        outs = [(d, c, n) for d, c, n in steps if c >= CC]
        ups = [(d, c, n) for d, c, n in steps if n < CH - 1]
        flat = lambda t: t[:, :, :].rearrange("p h t -> p (h t)")

        with nc.Block() as block:

            @block.tensor
            def _(pe):
                for c in range(QT):
                    for h in range(MH):
                        last = pe.matmul(K.ps[c % 2][:, h * P:h * P + P], M.k[:, h, c * P:c * P + P],
                                         M.q[:, h, c * P:c * P + P], start=True, stop=True)
                    last.then_inc(sem["qk"], 1)
                    if c < QT - 2:
                        pe.wait_ge(sem["qkk"], c + 1)
                def spread(o, rows, done):
                    d, c, n = outs[o]
                    for i in rows:
                        for h in range(MH):
                            last = pe.matmul(K.ps[i][:, h * P:h * P + P],
                                             const(K, "ident")[0:MH, h:h + 1].broadcast_to([MH, P]),
                                             M.bc[:, d, c, i, :], start=True, stop=True)
                    last.then_inc(done, 1)

                pe.wait_ge(sem["qkk"], QT)
                spread(0, (0, 1), sem["bc"])
                o = u = 0
                for d, c, n in steps:
                    if c >= CC:
                        if o >= 1:
                            pe.wait_ge(sem["h"], o)
                        spread(o, (2,), sem["bc2"])
                        pe.wait_ge(sem["s"], 2 * (o + 1))
                        if n >= 1:
                            pe.wait_ge(sem["st"], u + d + 1)
                        for h in range(MH):
                            pe.matmul(K.ps[3][:, h * P:h * P + P], C[:, h, 0:P], qs[:, h, :], start=True, stop=False)
                            pe.matmul(K.ps[3][:, h * P:h * P + P], M.v[:, c, h, 0:P], s_[:, h, :], start=False,
                                      stop=True)
                            pe.matmul(K.ps[4][:, h * P:h * P + P], C[:, h, P:P + 1].broadcast_to([P, P]), qs[:, h, :],
                                      start=True, stop=False)
                            last = pe.matmul(K.ps[4][:, h * P:h * P + P], K.ones[:, :], s_[:, h, :], start=False,
                                             stop=True)
                        last.then_inc(sem["nd"], 1)
                        o += 1
                        if o < len(outs):
                            spread(o, (0, 1), sem["bc"])
                    if n < CH - 1:
                        pe.wait_ge(sem["wk"], u + 1)
                        for h in range(MH):
                            last = pe.matmul(K.ps[5 + h // 2][:, (h % 2) * (P + 1):(h % 2 + 1) * (P + 1)],
                                             wk[:, h, :], M.v[:, c, h, :], start=True, stop=True)
                        last.then_inc(sem["u"], 1)
                        u += 1
                for h in range(MH):
                    pe.wait_ge(sem["sq"], h + 1)
                    pe.matmul(K.ps[h][:, :], K.ones[:, :], K.sq[:, h % 2, :], start=True, stop=True).then_inc(sem["ss"], 1)

            @block.scalar
            def _(act):
                for o, (d, c, n) in enumerate(outs):
                    act.wait_ge(sem["bc"], o + 1)
                    act.activation(K.ps[1][:, :], K.ps[1][:, :], ACT.Exp).then_inc(sem["ew"], 1)
                    act.wait_ge(sem["w"], o + 1)
                    for h in range(MH):
                        last = act.activation(w[:, h, :], w[:, h, :], ACT.Exp, bias=M.rw[:, d, c, 0, h:h + 1])
                    last.then_inc(sem["ew"], 1)
                    act.wait_ge(sem["bc2"], o + 1)
                    act.activation(K.ps[2][:, :], K.ps[2][:, :], ACT.Exp).then_inc(sem["ew"], 1)
                    act.wait_ge(sem["nd"], o + 1)
                    act.activation(flat(dn), K.ps[4][:, :], ACT.Abs).then_inc(sem["den"], 1)
                act.wait_ge(sem["h"], len(outs))
                for h in range(MH):
                    if h >= 2:
                        act.wait_ge(sem["ss"], h - 1)
                    act.activation(K.sq[:, h % 2, :], H[:, h, :], ACT.Square).then_inc(sem["sq"], 1)
                for h in range(MH):
                    act.wait_ge(sem["ss"], h + 1)
                    if h >= 2:
                        act.wait_ge(sem["hn"], h - 1)
                    act.activation(K.tmp[:, h % 2, :], K.ps[h][:, :], ACT.Sqrt, bias=K.eps[:, 0:1],
                                   scale=1.0 / P).then_inc(sem["sd"], 1)

            @block.vector
            def _(dve):
                link = lambda ins: K.dve.link(dve, ins)
                for c in range(QT):
                    dve.wait_ge(sem["qk"], c + 1)
                    dve.tensor_copy(qk[:, c].rearrange("p h t -> p (h t)"), K.ps[c % 2][:, :]).then_inc(sem["qkk"], 1)
                dve.wait_ge(sem["qkk"], QT)

                def gate_sum(o):
                    d = outs[o][0]
                    tri = const(K, "tri_f" if d == 0 else "tri_b").unsqueeze(1).broadcast_to([P, MH, P])
                    dve.wait_ge(sem["bc"], o + 1)
                    dve.tensor_tensor(w[:, :, :], K.ps[0][:, :].rearrange("p (h t) -> p h t", h=MH), tri,
                                      ALU.add).then_inc(sem["w"], 1)

                gate_sum(0)
                o = u = 0
                for d, c, n in steps:
                    if n == 0:
                        if d:
                            dve.wait_ge(sem["nd"], o)
                        dve.memset(C[:, :, :], 0.0).then_inc(sem["st"], 1)
                        dve.wait_ge(sem["st"], u + d + 1)
                    if c >= CC:
                        if o:
                            dve.wait_ge(sem["nd"], o)
                        dve.wait_ge(sem["ew"], 3 * o + 1)
                        t0 = (c - CC) * P
                        dve.tensor_tensor(qs[:, :, :], M.q[:, :, t0:t0 + P],
                                          K.ps[1][:, :].rearrange("p (h t) -> p h t", h=MH), ALU.mult).then_inc(sem["s"], 1)
                        dve.wait_ge(sem["ew"], 3 * o + 2)
                        dve.tensor_tensor(s_[:, :, :], qk[:, c - CC], w[:, :, :], ALU.mult).then_inc(sem["s"], 1)
                    if n < CH - 1:
                        if u:
                            dve.wait_ge(sem["u"], u)
                        wt = M.rw[:, d, c, 1, :].unsqueeze(2).broadcast_to([P, MH, P])
                        dve.tensor_tensor(wk[:, :, :], M.kr[:, c], wt, ALU.mult).then_inc(sem["wk"], 1)
                    if c >= CC:
                        if o + 1 < len(outs):
                            gate_sum(o + 1)
                        dve.wait_ge(sem["ew"], 3 * o + 3)
                        dve.wait_ge(sem["den"], o + 1)
                        link(dve.tensor_tensor(flat(dn), flat(dn), K.ps[2][:, :], ALU.max))
                        link(dve.reciprocal(flat(dn), flat(dn)))
                        hc = H[:, :, (c - CC) * P:(c - CC) * P + P]
                        num = K.ps[3][:, :].rearrange("p (h t) -> p h t", h=MH)
                        if d == 0:
                            dve.tensor_tensor(hc, num, dn[:, :, :], ALU.mult).then_inc(sem["h"], 1)
                        else:
                            link(dve.tensor_tensor(dn[:, :, :], num, dn[:, :, :], ALU.mult))
                            dve.tensor_tensor(hc, hc, dn[:, :, :], ALU.add).then_inc(sem["h"], 1)
                        o += 1
                    if n < CH - 1:
                        dve.wait_ge(sem["u"], u + 1)
                        if o:
                            dve.wait_ge(sem["nd"], o)
                        for h in range(MH):
                            last = dve.scalar_tensor_tensor(
                                C[:, h, :], C[:, h, :], M.oldc[:, h, d * CH + c:d * CH + c + 1],
                                K.ps[5 + h // 2][:, (h % 2) * (P + 1):(h % 2 + 1) * (P + 1)], ALU.mult, ALU.add)
                        last.then_inc(sem["st"], 1)
                        u += 1
                        dve.wait_ge(sem["st"], u + d + 1)
                for h in range(MH):
                    dve.wait_ge(sem["sd"], h + 1)
                    link(dve.reciprocal(K.tmp[:, h % 2, :], K.tmp[:, h % 2, :]))
                    link(dve.tensor_tensor(K.tmp[:, h % 2, :], K.tmp[:, h % 2, :], H[:, h, :], ALU.mult))
                    dve.scalar_tensor_tensor(K.h[:, h, CTX:TOK], K.tmp[:, h % 2, :], K.p("head_norm_2", h, 1),
                                             M.o[:, h, :], ALU.mult, ALU.mult).then_inc(sem["hn"], 1)


def stage_ffn_3(K, out):
    ffn(K, 2, False)
    rms_norms(K, [norm_out(lat(K.h), SEQ, K.coef[:, 11], lat(K.x))])


def stage_end(K, out):
    nc = K.nc
    turned, kept, stored = K.sem("end_turned"), K.sem("end_kept"), K.sem("end_stored")
    with ExitStack() as st, nc.Block() as block:
        o = K.sb("out_rows", [P, QT, D], st)

        @block.tensor
        def _(pe):
            for i in range(2 * QT):
                t, half = i // 2, i % 2
                if i >= 4:
                    pe.wait_ge(kept, i - 3)
                for k in range(4):
                    last = pe.transpose(K.ps[i % 4][:, k * P:k * P + P],
                                        K.x[:, 4 * half + k, CTX + t * P:CTX + t * P + P], const(K, "ident"))
                last.then_inc(turned, 1)

        @block.vector
        def _(dve):
            for i in range(2 * QT):
                t, half = i // 2, i % 2
                dve.wait_ge(turned, i + 1)
                dve.tensor_copy(o[:, t, 512 * half:512 * half + 512], K.ps[i % 4][:, :]).then_inc(kept, 1)

        @block.sync
        def _(sp):
            for t in range(QT):
                sp.wait_ge(kept, 2 * t + 2)
                sp.dma_start(out[0, t * P:t * P + P, :], o[:, t, :]).then_inc(stored, 16)
            sp.wait_ge(stored, 16 * QT)


def shape_constants():
    f = np.float32
    cst = np.zeros((P, NCONST), f)

    def put(name, a, rows=P):
        cst[0:rows, CONST[name][0]:CONST[name][1]] = a

    put("ident", np.eye(P, dtype=f))
    rot = np.zeros((P, P), f)
    half = ROPE // 2
    cos, sin = np.ones((P, SEQ), f), np.zeros((P, SEQ), f)
    inv = (1.0 / (np.float32(500000.0) ** (np.arange(0, ROPE, 2, dtype=f) / f(ROPE)))).astype(f)
    ang = np.arange(SEQ, dtype=f)[None, :] * inv[:, None]
    for base in (0, HD):
        for i in range(half):
            rot[base + half + i, base + i] = -1.0
            rot[base + i, base + half + i] = 1.0
            for r in (base + i, base + half + i):
                cos[r], sin[r] = np.cos(ang[i]), np.sin(ang[i])
    put("rot", rot)
    put("cos", cos)
    put("sin", sin)
    es = np.zeros((ROPE, 2, HD), f)
    es[:, :, 0:ROPE] = np.eye(ROPE, dtype=f)[:, None, :]
    put("esel", es.reshape(ROPE, P), ROPE)
    i = np.arange(P)
    causal = np.zeros((P, SEQ), f)
    causal[:, SEQ - P:] = np.where(i[None, :] <= i[:, None], 0, NEG)
    put("causal", causal)
    t = i[:, None, None] + P * np.arange(QT)[None, :, None]
    seen = (np.arange(NCMP) * 16 + 31)[None, None, :] <= t
    put("cmp_add", np.where(seen, 0, NEG).reshape(P, -1))
    put("cmp_one", seen.astype(f).reshape(P, -1))
    put("tri_f", np.where(i[:, None] <= i[None, :], 0, NEG))
    put("tri_b", np.where(i[:, None] >= i[None, :], 0, NEG))
    inv_count = np.zeros((4, SEQ // 64, 64), f)
    for g in range(4):
        win = 2 ** (g + 1)
        lo, hi = win // 2, win - 1 - win // 2

        def count(n):
            a = np.arange(n)
            return np.minimum(a + hi, n - 1) - np.maximum(a - lo, 0) + 1
        inv_count[g] = 1.0 / (count(SEQ // 64)[:, None] * count(64)[None, :])
    return cst, inv_count.reshape(1, -1)


_INS = ['x', 'c', 'w_ada', 'b_ada', 'g_pre_mix', 'g_post_mix', 'g_pre_ffn', 'g_post_ffn', 'w_in', 'cmp_pe', 'cmp_w1',
        'cmp_b1', 'cmp_w2', 'cmp_b2', 'g_kv_norm', 'w_uk', 'w_uv', 'w_out', 'w_gate_up', 'w_down', 'c_2', 'ctx_2',
        'c_ctx_2', 'w_mod_2', 'b_mod_2', 'norm_pre_2', 'norm_post_2', 'ffn_w_in_2', 'ffn_w_out_2', 'w_in_2', 'w_out_2',
        'conv_w_2', 'conv_b_2', 'w_q_2', 'w_k_2', 'i_bias_2', 'f_bias_2', 'head_norm_2', 'pool_w_2', 'pool_scale_2']


def kernel(**inputs):
    import concourse.bacc as bacc
    from concourse.bass_utils import run_bass_kernel_spmd

    nc = bacc.Bacc("TRN2", target_bir_lowering=False, num_devices=1)
    arrays = {f"in_{name}": np.ascontiguousarray(inputs[name]) for name in _INS}
    arrays["in_consts"], arrays["in_inv_count"] = shape_constants()
    A = {name[3:]: nc.dram_tensor(name, a.shape, mybir.dt.from_np(a.dtype), kind="ExternalInput").ap()
         for name, a in arrays.items()}
    out = nc.dram_tensor("out_0", (1, SEQ, D), F32, kind="ExternalOutput").ap()
    build(nc, A, out)
    r = run_bass_kernel_spmd(nc, [arrays], core_ids=[0])
    return r.results[0]["out_0"]
```
